# Optimizing a Trainium2 kernel written in Bass

```python
import math
import jax, jax.numpy as jnp
from jax import lax
import numpy as np
import jax
import jax.numpy as jnp

D_MODEL = 1024
BATCH = 1
SEQ = 256
DEPTH = 2

D_MIX = D_MODEL
DN_HEADS = 4
DN_HEAD_DIM = 128
DN_WIDTH = DN_HEADS * DN_HEAD_DIM
DN_CONV = 4
CHUNK = 64
SC_WIDTH = D_MIX - DN_WIDTH
SC_GROUPS = 4
SC_GROUP_DIM = SC_WIDTH // SC_GROUPS
SC_CONV = 3
D_FF = ((8 * D_MODEL + 3 * 256 - 1) // (3 * 256)) * 256
W_IN_COLS = 4 * DN_WIDTH + 2 * DN_HEADS + 3 * SC_WIDTH
EPS = 1e-6


def rms_norm(x, gain):
    xf = x.astype(jnp.float32)
    y = xf * lax.rsqrt(jnp.mean(xf * xf, axis=-1, keepdims=True) + EPS)
    return (y * gain.astype(jnp.float32)).astype(x.dtype)

def l2_normalize(x):
    return x * lax.rsqrt(jnp.sum(x * x, axis=-1, keepdims=True) + EPS)

def causal_depthwise_conv(x, w):
    K = w.shape[0]
    T = x.shape[1]
    xp = jnp.pad(x, ((0, 0), (K - 1, 0), (0, 0)))
    y = xp[:, 0:T, :] * w[0]
    for j in range(1, K):
        y = y + xp[:, j:j + T, :] * w[j]
    return y

def chunk_gated_delta_rule(q, k, v, g, beta):
    Bsz, T, H, DK = q.shape
    DV = v.shape[-1]
    C = CHUNK
    N = T // C
    q = q * (DK ** -0.5)

    def to_chunks(t):
        return t.reshape(Bsz, N, C, H, t.shape[-1]).transpose(0, 3, 1, 2, 4)

    q, k, v = to_chunks(q), to_chunks(k), to_chunks(v)
    g = jnp.cumsum(g.reshape(Bsz, N, C, H).transpose(0, 3, 1, 2), axis=-1)
    beta = beta.reshape(Bsz, N, C, H).transpose(0, 3, 1, 2)

    causal = jnp.tril(jnp.ones((C, C), dtype=bool))
    strict = jnp.tril(jnp.ones((C, C), dtype=bool), -1)
    decay = jnp.exp(jnp.where(causal, g[..., :, None] - g[..., None, :], -jnp.inf))

    k_beta = k * beta[..., None]
    v_beta = v * beta[..., None]
    lower = jnp.where(strict, jnp.einsum('bhncd,bhnmd->bhncm', k_beta, k) * decay, 0.0)
    a_mat = lower + jnp.eye(C, dtype=jnp.float32)
    rhs = jnp.concatenate([v_beta, k_beta * jnp.exp(g)[..., None]], axis=-1)
    sol = lax.linalg.triangular_solve(a_mat, rhs, left_side=True, lower=True, unit_diagonal=True)
    u, w = sol[..., :DV], sol[..., DV:]

    qk = jnp.einsum('bhncd,bhnmd->bhncm', q, k) * decay
    q_dec = q * jnp.exp(g)[..., None]
    k_dec = k * jnp.exp(g[..., -1:] - g)[..., None]
    g_last = jnp.exp(g[..., -1])

    def step(S, xs):
        qk_i, q_dec_i, k_dec_i, u_i, w_i, gl_i = xs
        v_new = u_i - jnp.einsum('bhck,bhkv->bhcv', w_i, S)
        o_i = jnp.einsum('bhck,bhkv->bhcv', q_dec_i, S) + jnp.einsum('bhcm,bhmv->bhcv', qk_i, v_new)
        S = S * gl_i[..., None, None] + jnp.einsum('bhck,bhcv->bhkv', k_dec_i, v_new)
        return S, o_i

    xs = (jnp.moveaxis(qk, 2, 0), jnp.moveaxis(q_dec, 2, 0), jnp.moveaxis(k_dec, 2, 0),
          jnp.moveaxis(u, 2, 0), jnp.moveaxis(w, 2, 0), jnp.moveaxis(g_last, 2, 0))
    S0 = jnp.zeros((Bsz, H, DK, DV), dtype=jnp.float32)
    _, o = lax.scan(step, S0, xs)
    return o.transpose(1, 0, 3, 2, 4).reshape(Bsz, T, H, DV)

def hybrid_layer(x, norm1_g, w_in, dn_conv_w, dn_a_log, dn_dt_bias, dn_norm_g,
                 sc_conv_w, sc_norm_g, w_out, norm2_g, ffn_w_gate, ffn_w_up, ffn_w_down):
    Bsz, T, _ = x.shape
    h = rms_norm(x, norm1_g)
    proj = h @ w_in
    o1 = 3 * DN_WIDTH
    o2 = o1 + DN_WIDTH
    o3 = o2 + DN_HEADS
    o4 = o3 + DN_HEADS
    qkv, z, b_in, a_in, sc_in = proj[..., :o1], proj[..., o1:o2], proj[..., o2:o3], proj[..., o3:o4], proj[..., o4:]

    qkv = jax.nn.silu(causal_depthwise_conv(qkv, dn_conv_w)).astype(jnp.float32)
    q = l2_normalize(qkv[..., :DN_WIDTH].reshape(Bsz, T, DN_HEADS, DN_HEAD_DIM))
    k = l2_normalize(qkv[..., DN_WIDTH:2 * DN_WIDTH].reshape(Bsz, T, DN_HEADS, DN_HEAD_DIM))
    v = qkv[..., 2 * DN_WIDTH:].reshape(Bsz, T, DN_HEADS, DN_HEAD_DIM)
    beta = jax.nn.sigmoid(b_in.astype(jnp.float32))
    g = -jnp.exp(dn_a_log.astype(jnp.float32)) * jax.nn.softplus(
        a_in.astype(jnp.float32) + dn_dt_bias.astype(jnp.float32))
    o_dn = chunk_gated_delta_rule(q, k, v, g, beta)
    zf = z.astype(jnp.float32).reshape(Bsz, T, DN_HEADS, DN_HEAD_DIM)
    o_dn = (o_dn * lax.rsqrt(jnp.mean(o_dn * o_dn, axis=-1, keepdims=True) + EPS)
            * dn_norm_g.astype(jnp.float32) * jax.nn.silu(zf))
    o_dn = o_dn.reshape(Bsz, T, DN_WIDTH).astype(x.dtype)

    gate_b, gate_c, hv = sc_in[..., :SC_WIDTH], sc_in[..., SC_WIDTH:2 * SC_WIDTH], sc_in[..., 2 * SC_WIDTH:]
    y = gate_b * causal_depthwise_conv(gate_c * hv, sc_conv_w)
    yf = y.astype(jnp.float32).reshape(Bsz, T, SC_GROUPS, SC_GROUP_DIM)
    yf = yf * lax.rsqrt(jnp.mean(yf * yf, axis=-1, keepdims=True) + EPS)
    o_sc = (yf * sc_norm_g.astype(jnp.float32).reshape(SC_GROUPS, SC_GROUP_DIM)).reshape(Bsz, T, SC_WIDTH).astype(x.dtype)

    x = x + jnp.concatenate([o_dn, o_sc], axis=-1) @ w_out

    h2 = rms_norm(x, norm2_g)
    x = x + (jax.nn.silu(h2 @ ffn_w_gate) * (h2 @ ffn_w_up)) @ ffn_w_down
    return x

def first_inputs(seed: int = 0) -> dict:
    key = jax.random.key(seed)
    ks = jax.random.split(key, 16)
    f32 = jnp.float32

    def nrm(k, shape, scale):
        return jax.random.normal(k, shape, f32) * scale

    def gain(k, shape):
        return 1.0 + 0.02 * jax.random.normal(k, shape, f32)

    x = nrm(ks[0], (BATCH, SEQ, D_MODEL), 1.0)
    norm1_g = gain(ks[1], (DEPTH, D_MODEL))
    w_in = nrm(ks[2], (DEPTH, D_MODEL, W_IN_COLS), D_MODEL ** -0.5)
    dn_conv_w = nrm(ks[3], (DEPTH, DN_CONV, 3 * DN_WIDTH), DN_CONV ** -0.5)
    dn_a_log = jnp.log(jax.random.uniform(ks[4], (DEPTH, DN_HEADS), f32, 1.0, 16.0))
    dt = jnp.exp(jax.random.uniform(ks[5], (DEPTH, DN_HEADS), f32, math.log(1e-3), math.log(1e-1)))
    dn_dt_bias = dt + jnp.log(-jnp.expm1(-dt))
    dn_norm_g = gain(ks[6], (DEPTH, DN_HEAD_DIM))
    sc_conv_w = nrm(ks[7], (DEPTH, SC_CONV, SC_WIDTH), SC_CONV ** -0.5)
    sc_norm_g = gain(ks[8], (DEPTH, SC_WIDTH))
    w_out = nrm(ks[9], (DEPTH, D_MIX, D_MODEL), D_MIX ** -0.5)
    norm2_g = gain(ks[10], (DEPTH, D_MODEL))
    ffn_w_gate = nrm(ks[11], (DEPTH, D_MODEL, D_FF), D_MODEL ** -0.5)
    ffn_w_up = nrm(ks[12], (DEPTH, D_MODEL, D_FF), D_MODEL ** -0.5)
    ffn_w_down = nrm(ks[13], (DEPTH, D_FF, D_MODEL), D_FF ** -0.5)
    final_norm_g = gain(ks[14], (D_MODEL,))
    return {'x': x, 'norm1_g': norm1_g, 'w_in': w_in, 'dn_conv_w': dn_conv_w,
            'dn_a_log': dn_a_log, 'dn_dt_bias': dn_dt_bias, 'dn_norm_g': dn_norm_g,
            'sc_conv_w': sc_conv_w, 'sc_norm_g': sc_norm_g, 'w_out': w_out,
            'norm2_g': norm2_g, 'ffn_w_gate': ffn_w_gate, 'ffn_w_up': ffn_w_up,
            'ffn_w_down': ffn_w_down, 'final_norm_g': final_norm_g}

def first_block(x, norm1_g, w_in, dn_conv_w, dn_a_log, dn_dt_bias, dn_norm_g, sc_conv_w,
              sc_norm_g, w_out, norm2_g, ffn_w_gate, ffn_w_up, ffn_w_down, final_norm_g):
    for l in range(DEPTH):
        x = hybrid_layer(x, norm1_g[l], w_in[l], dn_conv_w[l], dn_a_log[l], dn_dt_bias[l],
                         dn_norm_g[l], sc_conv_w[l], sc_norm_g[l], w_out[l], norm2_g[l],
                         ffn_w_gate[l], ffn_w_up[l], ffn_w_down[l])
    return rms_norm(x, final_norm_g)


GRID_W = 64
CTX_LEN = 256
HEAD_DIM = 128
N_HEADS = D_MODEL // HEAD_DIM
N_KV_HEADS = N_HEADS // 4
Q_GROUP = N_HEADS // N_KV_HEADS
Q_BLOCK = 128
ATTN_SCALE = HEAD_DIM ** -0.5
ROPE_THETA = 10000.0
ROPE_PAIRS = HEAD_DIM // 4
CONV_WIDTH = 31
CONV_CH = D_MODEL
POOL_WINDOWS = (2, 4, 8, 16)
POOL_GROUPS = len(POOL_WINDOWS)
POOL_CH = D_MODEL
POOL_GROUP_CH = POOL_CH // POOL_GROUPS
N_BRANCH = 3
D_FF_2 = 2816
FFN_CONV_WIDTH = 3
N_MOD = 6
ATTN_W = N_HEADS * HEAD_DIM
KV_W = N_KV_HEADS * HEAD_DIM
Q_END = ATTN_W
K_END = Q_END + KV_W
V_END = K_END + KV_W
CONV_END = V_END + 2 * CONV_CH
POOL_END = CONV_END + POOL_CH
D_IN = POOL_END + N_BRANCH * D_MODEL
DEEPNORM_ALPHA = (2 * DEPTH) ** 0.25
DEEPNORM_BETA = (8 * DEPTH) ** -0.25
LN_EPS = 1e-5
RMS_EPS = 1e-6


def layer_norm(t, g, b):
    tf = t.astype(jnp.float32)
    mu = jnp.mean(tf, axis=-1, keepdims=True)
    var = jnp.mean(jnp.square(tf - mu), axis=-1, keepdims=True)
    return ((tf - mu) * lax.rsqrt(var + LN_EPS)).astype(t.dtype) * g + b

def rms_norm_2(t, g):
    tf = t.astype(jnp.float32)
    ms = jnp.mean(jnp.square(tf), axis=-1, keepdims=True)
    return (tf * lax.rsqrt(ms + RMS_EPS)).astype(t.dtype) * g

def ada_mod(cond, w, b, n):
    m = jax.nn.silu(cond) @ w[:, :n * D_MODEL] + b[:n * D_MODEL]
    return m.reshape(m.shape[:-1] + (n, D_MODEL))

def modulate(h, shift, scale):
    return h * (1.0 + scale) + shift

def axial_rope_tables(n_tokens):
    n_rows = n_tokens // GRID_W
    row = jnp.repeat(jnp.arange(n_rows, dtype=jnp.float32), GRID_W)
    col = jnp.tile(jnp.arange(GRID_W, dtype=jnp.float32), n_rows)
    inv_freq = ROPE_THETA ** (-jnp.arange(ROPE_PAIRS, dtype=jnp.float32) / ROPE_PAIRS)
    ang = jnp.stack([row, col], axis=-1)[..., None] * inv_freq
    return jnp.cos(ang), jnp.sin(ang)

def apply_rope(t, cos, sin):
    b, n, h, _ = t.shape
    tf = t.astype(jnp.float32).reshape(b, n, h, 2, 2, ROPE_PAIRS)
    t1, t2 = tf[..., 0, :], tf[..., 1, :]
    c = cos[None, :, None]
    s = sin[None, :, None]
    out = jnp.stack([t1 * c - t2 * s, t1 * s + t2 * c], axis=-2)
    return out.reshape(t.shape).astype(t.dtype)

def kv_heads(z_kv, k_gain):
    lead = z_kv.shape[:-1]
    k = rms_norm_2(z_kv[..., :KV_W].reshape(lead + (N_KV_HEADS, HEAD_DIM)), k_gain)
    v = z_kv[..., KV_W:].reshape(lead + (N_KV_HEADS, HEAD_DIM))
    return k, v

def qkv_heads(z, q_gain, k_gain):
    q = rms_norm_2(z[..., :Q_END].reshape(z.shape[:-1] + (N_HEADS, HEAD_DIM)), q_gain)
    k, v = kv_heads(z[..., Q_END:V_END], k_gain)
    return q, k, v

def latent_attention(q, k_lat, v_lat, k_ctx, v_ctx):
    b, n = q.shape[0], q.shape[1]
    k_all = jnp.concatenate([k_ctx, k_lat], axis=1)
    v_all = jnp.concatenate([v_ctx, v_lat], axis=1)
    n_blk = n // Q_BLOCK
    qb = jnp.moveaxis(q.reshape(b, n_blk, Q_BLOCK, N_KV_HEADS, Q_GROUP, HEAD_DIM), 1, 0)

    def block(qi):
        s = jnp.einsum('bqhgd,bkhd->bhgqk', qi, k_all, preferred_element_type=jnp.float32) * ATTN_SCALE
        p = jax.nn.softmax(s, axis=-1).astype(v_all.dtype)
        return jnp.einsum('bhgqk,bkhd->bqhgd', p, v_all)

    o = lax.map(block, qb)
    return jnp.moveaxis(o, 0, 1).reshape(b, n, ATTN_W)

def context_attention(q, k, v):
    b, n = q.shape[0], q.shape[1]
    qg = q.reshape(b, n, N_KV_HEADS, Q_GROUP, HEAD_DIM)
    s = jnp.einsum('bqhgd,bkhd->bhgqk', qg, k, preferred_element_type=jnp.float32) * ATTN_SCALE
    p = jax.nn.softmax(s, axis=-1).astype(v.dtype)
    return jnp.einsum('bhgqk,bkhd->bqhgd', p, v).reshape(b, n, ATTN_W)

def depthwise_conv(t, w, b):
    k = w.shape[0]
    y = lax.conv_general_dilated(
        t, w[:, None, :], window_strides=(1,), padding=[((k - 1) // 2, k // 2)],
        dimension_numbers=('NWC', 'WIO', 'NWC'), feature_group_count=t.shape[-1])
    return y + b

def conformer_conv(u, dw_w, dw_b, ln_g, ln_b, pw_w, pw_b):
    a, gt = jnp.split(u, 2, axis=-1)
    h = depthwise_conv(a * jax.nn.sigmoid(gt), dw_w, dw_b)
    h = jax.nn.silu(layer_norm(h, ln_g, ln_b))
    return h @ pw_w + pw_b

def multiscale_pool(u, pool_w, pool_scale):
    b, n, _ = u.shape
    uf = u.astype(jnp.float32)
    cs = jnp.pad(jnp.cumsum(uf, axis=1), ((0, 0), (1, 0), (0, 0)))
    t = jnp.arange(n)
    outs = []
    for g, w in enumerate(POOL_WINDOWS):
        lo = jnp.clip(t - w // 2, 0, n)
        hi = jnp.clip(t - w // 2 + w, 0, n)
        sl = slice(g * POOL_GROUP_CH, (g + 1) * POOL_GROUP_CH)
        seg = cs[:, :, sl]
        win_sum = jnp.take(seg, hi, axis=1) - jnp.take(seg, lo, axis=1)
        cnt = (hi - lo).astype(jnp.float32)[None, :, None]
        outs.append(win_sum / cnt - uf[:, :, sl])
    pooled = jnp.stack(outs, axis=2).astype(u.dtype)
    mixed = jnp.einsum('blgi,gio->blgo', pooled, pool_w)
    return mixed.reshape(b, n, POOL_CH) * pool_scale

def merge_branches(z, attn_o, conv_dw_w, conv_dw_b, conv_ln_g, conv_ln_b, conv_pw_w, conv_pw_b,
                   pool_w, pool_scale, w_out, b_out):
    conv_o = conformer_conv(z[..., V_END:CONV_END], conv_dw_w, conv_dw_b, conv_ln_g, conv_ln_b,
                            conv_pw_w, conv_pw_b)
    pool_o = multiscale_pool(z[..., CONV_END:POOL_END], pool_w, pool_scale)
    gates = jax.nn.sigmoid(z[..., POOL_END:].reshape(z.shape[:-1] + (N_BRANCH, D_MODEL)))
    m = gates[..., 0, :] * attn_o + gates[..., 1, :] * conv_o + gates[..., 2, :] * pool_o
    return m @ w_out + b_out

def conv_ffn(h, w_up, dw_w, dw_b, w_down):
    a, u = jnp.split(h @ w_up, 2, axis=-1)
    a = depthwise_conv(a, dw_w, dw_b)
    return (jax.nn.silu(a) * u) @ w_down

def second_inputs(seed: int = 0) -> dict:
    key = jax.random.key(seed)
    ks = iter(jax.random.split(key, 32))

    def nrm(shape, scale):
        return jax.random.normal(next(ks), shape, jnp.float32) * scale

    L = DEPTH
    D = D_MODEL
    return {
        'x': nrm((BATCH, SEQ, D), 1.0),
        'c': nrm((BATCH, D), 1.0),
        'ctx': nrm((BATCH, CTX_LEN, D), 1.0),
        'c_ctx': nrm((D,), 1.0),
        'w_ada': nrm((L, D, N_MOD * D), 0.5 * D ** -0.5),
        'b_ada': nrm((L, N_MOD * D), 0.02),
        'w_in': nrm((L, D, D_IN), D ** -0.5),
        'b_in': nrm((L, D_IN), 0.02),
        'q_gain': 1.0 + nrm((L, HEAD_DIM), 0.02),
        'k_gain': 1.0 + nrm((L, HEAD_DIM), 0.02),
        'conv_dw_w': nrm((L, CONV_WIDTH, CONV_CH), CONV_WIDTH ** -0.5),
        'conv_dw_b': nrm((L, CONV_CH), 0.02),
        'conv_ln_g': 1.0 + nrm((L, CONV_CH), 0.02),
        'conv_ln_b': nrm((L, CONV_CH), 0.02),
        'conv_pw_w': nrm((L, CONV_CH, D), CONV_CH ** -0.5),
        'conv_pw_b': nrm((L, D), 0.02),
        'pool_w': nrm((L, POOL_GROUPS, POOL_GROUP_CH, POOL_GROUP_CH), POOL_GROUP_CH ** -0.5),
        'pool_scale': 1.0 + nrm((L, POOL_CH), 0.1),
        'w_out': nrm((L, D, D), DEEPNORM_BETA * D ** -0.5),
        'b_out': nrm((L, D), 0.02),
        'ln1_g': 1.0 + nrm((L, D), 0.02),
        'ln1_b': nrm((L, D), 0.02),
        'ln2_g': 1.0 + nrm((L, D), 0.02),
        'ln2_b': nrm((L, D), 0.02),
        'w_up': nrm((L, D, 2 * D_FF_2), D ** -0.5),
        'ffn_dw_w': nrm((L, FFN_CONV_WIDTH, D_FF_2), FFN_CONV_WIDTH ** -0.5),
        'ffn_dw_b': nrm((L, D_FF_2), 0.02),
        'w_down': nrm((L, D_FF_2, D), DEEPNORM_BETA * D_FF_2 ** -0.5),
    }

def second_block(x, c, ctx, c_ctx, w_ada, b_ada, w_in, b_in, q_gain, k_gain,
              conv_dw_w, conv_dw_b, conv_ln_g, conv_ln_b, conv_pw_w, conv_pw_b,
              pool_w, pool_scale, w_out, b_out, ln1_g, ln1_b, ln2_g, ln2_b,
              w_up, ffn_dw_w, ffn_dw_b, w_down):
    cos, sin = axial_rope_tables(x.shape[1])
    for l in range(DEPTH):
        last = l == DEPTH - 1

        def mix(z, attn_o):
            return merge_branches(z, attn_o, conv_dw_w[l], conv_dw_b[l], conv_ln_g[l], conv_ln_b[l],
                                  conv_pw_w[l], conv_pw_b[l], pool_w[l], pool_scale[l],
                                  w_out[l], b_out[l])

        def ffn(h):
            return conv_ffn(h, w_up[l], ffn_dw_w[l], ffn_dw_b[l], w_down[l])

        ml = ada_mod(c, w_ada[l], b_ada[l], N_MOD)[:, None]
        mc = ada_mod(c_ctx, w_ada[l], b_ada[l], 2 if last else N_MOD)

        hl = modulate(x, ml[..., 0, :], ml[..., 1, :])
        hc = modulate(ctx, mc[0], mc[1])
        zl = hl @ w_in[l] + b_in[l]
        q_l, k_l, v_l = qkv_heads(zl, q_gain[l], k_gain[l])
        q_l = apply_rope(q_l, cos, sin)
        k_l = apply_rope(k_l, cos, sin)
        if last:
            k_c, v_c = kv_heads(hc @ w_in[l][:, Q_END:V_END] + b_in[l][Q_END:V_END], k_gain[l])
        else:
            zc = hc @ w_in[l] + b_in[l]
            q_c, k_c, v_c = qkv_heads(zc, q_gain[l], k_gain[l])
        attn_l = latent_attention(q_l, k_l, v_l, k_c, v_c)
        x = layer_norm(DEEPNORM_ALPHA * x + ml[..., 2, :] * mix(zl, attn_l), ln1_g[l], ln1_b[l])

        x = layer_norm(DEEPNORM_ALPHA * x + ml[..., 5, :] * ffn(modulate(x, ml[..., 3, :], ml[..., 4, :])),
                       ln2_g[l], ln2_b[l])

        if not last:
            attn_c = context_attention(q_c, k_c, v_c)
            ctx = layer_norm(DEEPNORM_ALPHA * ctx + mc[2] * mix(zc, attn_c), ln1_g[l], ln1_b[l])
            ctx = layer_norm(DEEPNORM_ALPHA * ctx + mc[5] * ffn(modulate(ctx, mc[3], mc[4])),
                             ln2_g[l], ln2_b[l])
    return x


def setup_inputs(seed=0):
    out = dict(first_inputs(seed))
    for name, value in second_inputs(seed + 1).items():
        if name != "x":
            out[name + "_2"] = value
    return out


def reference(
    x, norm1_g, w_in, dn_conv_w, dn_a_log, dn_dt_bias, dn_norm_g, sc_conv_w, sc_norm_g, w_out,
    norm2_g, ffn_w_gate, ffn_w_up, ffn_w_down, final_norm_g, c_2, ctx_2, c_ctx_2, w_ada_2,
    b_ada_2, w_in_2, b_in_2, q_gain_2, k_gain_2, conv_dw_w_2, conv_dw_b_2, conv_ln_g_2,
    conv_ln_b_2, conv_pw_w_2, conv_pw_b_2, pool_w_2, pool_scale_2, w_out_2, b_out_2, ln1_g_2,
    ln1_b_2, ln2_g_2, ln2_b_2, w_up_2, ffn_dw_w_2, ffn_dw_b_2, w_down_2,
):
    x = first_block(
        x, norm1_g, w_in, dn_conv_w, dn_a_log, dn_dt_bias, dn_norm_g, sc_conv_w, sc_norm_g,
        w_out, norm2_g, ffn_w_gate, ffn_w_up, ffn_w_down, final_norm_g,
    )
    return second_block(
        x, c_2, ctx_2, c_ctx_2, w_ada_2, b_ada_2, w_in_2, b_in_2, q_gain_2, k_gain_2,
        conv_dw_w_2, conv_dw_b_2, conv_ln_g_2, conv_ln_b_2, conv_pw_w_2, conv_pw_b_2, pool_w_2,
        pool_scale_2, w_out_2, b_out_2, ln1_g_2, ln1_b_2, ln2_g_2, ln2_b_2, w_up_2, ffn_dw_w_2,
        ffn_dw_b_2, w_down_2,
    )


_drawn_inputs = setup_inputs


def setup_inputs(seed=0):
    import zlib

    import numpy as np

    out = dict(_drawn_inputs(seed))
    spreads = {}
    factors = {'dn_norm_g': 5.152,
     'sc_norm_g': 3.256,
     'norm2_g': 3.066,
     'final_norm_g': 2.856,
     'ctx_2': 8.0,
     'c_ctx_2': 4.547,
     'b_ada_2': 5.207,
     'b_in_2': 8.0,
     'q_gain_2': 8.0,
     'k_gain_2': 8.0,
     'conv_dw_b_2': 8.0,
     'conv_ln_g_2': 61.652,
     'conv_ln_b_2': 64.0,
     'conv_pw_b_2': 45.429,
     'pool_scale_2': 7.33,
     'b_out_2': 32.426,
     'ffn_dw_b_2': 23.899}
    for name, (base, spread) in spreads.items():
        noise = np.random.default_rng([zlib.crc32(name.encode()), seed]).standard_normal(out[name].shape)
        drawn = base * np.exp(spread * noise) if base else spread * noise
        out[name] = jnp.asarray(drawn.astype(out[name].dtype))
    for name, factor in factors.items():
        out[name] = (out[name] * factor).astype(out[name].dtype)
    return out
```

```python
from contextlib import ExitStack

import concourse.bass as bass
from concourse import mybir
import numpy as np

F32 = mybir.dt.float32
ALU = mybir.AluOpType
ACT = mybir.ActivationFunctionType
AX = mybir.AxisListType

P = 128
D = 1024
KD = D // P
SEQ = 256
CTX = 256
TOK = SEQ + CTX
DEPTH = 2
EPS = 1e-6
LN_EPS = 1e-5

HEADS = 4
CONV = 4
SC_CONV = 3
D_FF = 2816
KF = D_FF // P
W_IN_COLS = 3592
B_AT, SC_AT = 2048, 2056
NE = 2 * HEADS

N_HEADS, KV_HEADS = 8, 2
CW = 31
CPAD = CW // 2
POOLS = (2, 4, 8, 16)
PPAD = max(POOLS) // 2
D_IN = 7680
Q_AT, CONV_AT, GATE_AT, POOL_AT, MIX_AT = 0, 1536, 2560, 3584, 4608
ATTN_SCALE = P ** -0.5
ALPHA = (2 * DEPTH) ** 0.25
GRID_W = 64
ROPE_THETA = 10000.0
N_MOD = 6

PC = 256
SLOTS = 3
BANKS = 4
N_ADA = N_MOD * D // PC
ADA_BANKS = 3
KPARTS = ((0, 8), (8, 8), (16, 6))

P1_BA, P1_QKV, P1_Z, P1_GC, P1_HV, P1_GB, P1_ADA, P1_OUT, P1_FFN, P1_DOWN, P1_ALL = (
    0, 2, 8, 10, 12, 14, 16, 40, 44, 66, 78)
C1_QKV, C1_Z, C1_GC, C1_HV, C1_GB, C1_OUT, C1_FFN, C1_DOWN, C1_ALL = 0, 12, 16, 20, 24, 28, 36, 80, 88
P2_CONV, P2_QKV, P2_POOL, P2_G0, P2_PMIX, P2_G2, P2_PW, P2_G1, P2_OUT, P2_FFN, P2_DOWN, P2_ALL = (
    0, 8, 14, 18, 22, 26, 30, 34, 38, 42, 64, 76)
C2_CONV, C2_QKV, C2_POOL, C2_G0, C2_PMIX, C2_G2, C2_PW, C2_G1, C2_OUT, C2_FFN, C2_DOWN, C2_ALL = (
    0, 16, 28, 36, 44, 52, 60, 68, 76, 84, 128, 136)
P2_AT, C2_AT = DEPTH * P1_ALL, DEPTH * C1_ALL
assert P1_ALL % SLOTS == 0 and C1_ALL % BANKS == 0 and C2_ALL % BANKS == 0

N1_IN, N1_L2, N1_MIX, N1_FFN, N1_ALL = 0, 1, 2, 3, 4
N_FINAL = DEPTH * N1_ALL

V1 = {}
for _name, _n in (("norm1", 8), ("dnw", 48), ("scw", 12), ("dng", 1), ("scg", 4), ("norm2", 8),
                  ("alog", 4), ("dtb", 4), ("ada", 48)):
    V1[_name] = sum(n for _, n in V1.values()), _n
V1_N = sum(n for _, n in V1.values())
V2 = {}
for _name, _n in (("bin", 60), ("qg", 1), ("kg", 1), ("cw", CW * KD), ("cb", 8), ("clg", 8),
                  ("clb", 8), ("pwb", 8), ("psc", 8), ("bout", 8), ("l1g", 8), ("l1b", 8), ("l2g", 8),
                  ("l2b", 8), ("fw", 3 * KF), ("fb", KF)):
    V2[_name] = sum(n for _, n in V2.values()), _n
V2_N = sum(n for _, n in V2.values())
LEVELS = 7
TAB = {}
for _name, _n in (("ident", P), ("upper", P), ("cap", P), ("level", LEVELS * P), ("perm", P), ("cos", SEQ),
                  ("sin", SEQ), ("cnt", len(POOLS) * SEQ), ("one", 1), ("inv_d", 1), ("inv_p", 1), ("eps", 1),
                  ("ln_eps", 1)):
    TAB[_name] = sum(n for _, n in TAB.values()), _n
TAB_N = sum(n for _, n in TAB.values())


def tables():
    m, c = np.meshgrid(np.arange(P), np.arange(P), indexing="ij")
    t = np.arange(SEQ)
    out = {"ident": (m == c), "upper": (m <= c), "cap": np.where(m <= c, 0.0, -3e38)}
    out["level"] = np.concatenate(
        [(m // (2 << s) == c // (2 << s)) & (m % (2 << s) < (1 << s)) & (c % (2 << s) >= (1 << s))
         for s in range(LEVELS)], axis=1)
    half = (c // 32) % 2
    out["perm"] = np.where((half == 0) & (m == c + 32), -1.0, 0.0) + np.where((half == 1) & (m == c - 32), 1.0, 0.0)
    pairs = P // 4
    inv = np.float32(ROPE_THETA) ** (-np.arange(pairs, dtype=np.float32) / np.float32(pairs))
    row, col = (t // GRID_W).astype(np.float32), (t % GRID_W).astype(np.float32)
    ang = np.stack([np.outer(inv, row), np.outer(inv, col)]).astype(np.float32)
    ang = np.repeat(ang[:, None], 2, axis=1).reshape(P, SEQ)
    out["cos"], out["sin"] = np.cos(ang), np.sin(ang)
    cnt = np.stack([np.clip(t - w // 2 + w, 0, SEQ) - np.clip(t - w // 2, 0, SEQ) for w in POOLS])
    out["cnt"] = np.broadcast_to((1.0 / cnt).reshape(1, -1), (P, len(POOLS) * SEQ))
    for name, v in (("one", 1.0), ("inv_d", 1.0 / D), ("inv_p", 1.0 / P), ("eps", EPS), ("ln_eps", LN_EPS)):
        out[name] = np.full((P, 1), v)
    return np.concatenate([out[n].astype(np.float32) for n in TAB], axis=1)


class Order:

    def __init__(self, eng, sem):
        self.eng, self.sem, self.base, self.n, self.outer = eng, sem, 0, 0, []

    def __call__(self, ins):
        self.n += 1
        ins.then_inc(self.sem, 1)
        return self.n

    def wait(self, step=None):
        self.eng.wait_ge(self.sem, self.base + (step or self.n))

    def enter(self, i, steps, first=0):
        self.outer.append((self.base, self.n, steps))
        self.base = i * steps + (self.base - first * steps)

    def leave(self, turns):
        base, n, steps = self.outer.pop()
        assert self.n - n == steps, ("steps of a turn", self.n - n, steps)
        self.base, self.n = base, n + steps * turns


def flat(v):
    return v.rearrange("p a b -> p (a b)")


def build(nc, x, ctx_in, cond, vec1, vec_final, vec2, tabs, w_in, w_out, w_gate, w_up, w_down,
          w_ada, w_in2, w_pool, w_pw, w_out2, w_up2, w_down2, out):
    with ExitStack() as ctx:
        def sb(name, cols):
            return ctx.enter_context(nc.sbuf_tensor(name, [P, cols], F32))

        def sem(name):
            return ctx.enter_context(nc.semaphore(name))

        W = sb("W", SLOTS * KD * PC)[:, :].rearrange("p (s k n) -> p s k n", s=SLOTS, k=KD)
        X = sb("X", KD * TOK)[:, :].rearrange("p (k t) -> p k t", k=KD)
        Hn = sb("Hn", KD * TOK)[:, :].rearrange("p (k t) -> p k t", k=KD)
        tab = sb("tab", TAB_N)
        p1 = sb("p1", V1_N)
        pf = sb("pf", KD)
        p2 = sb("p2", DEPTH * V2_N)
        cnd = sb("cnd", KD * 2)[:, :].rearrange("p (k c) -> p k c", c=2)
        mods = sb("mods", DEPTH * N_MOD * KD * 2)
        small = sb("small", 192)
        roots, scales, rates = small[:, 0:40], small[:, 40:80], small[:, 80:84]
        ARENA = 28100
        arena = sb("arena", ARENA)
        ps = ctx.enter_context(nc.psum_tensor("ps", [P, 8, 512], F32))

        at = [0]

        def take(*dims):
            n = int(np.prod(dims))
            v = arena[:, at[0]:at[0] + n]
            at[0] += n
            assert at[0] <= ARENA, at[0]
            if len(dims) == 2:
                v = v.rearrange("p (a b) -> p a b", b=dims[1])
            if len(dims) == 3:
                v = v.rearrange("p (a b c) -> p a b c", b=dims[1], c=dims[2])
            return v

        def T(name, i=0, n=None):
            a, m = TAB[name]
            return tab[:, a + i:a + i + (n or m)]

        def v1(name, i=0, n=1):
            return p1[:, V1[name][0] + i:V1[name][0] + i + n]

        def v2(L, name, i=0, n=1):
            return p2[:, bass.ds(L * V2_N + V2[name][0] + i, n)]

        ident = T("ident")

        def ada_rows(jj):
            return xpad[0:2, jj % 12, CONV - 1:]

        X1, H1 = X[:, :, 0:SEQ], Hn[:, :, 0:SEQ]
        mix1, sq1 = Hn[:, :, SEQ:TOK], X[:, :, SEQ:TOK]
        ktok = take(NE, P)
        vtok = take(NE, P)
        DT = take(NE, P)
        AT = take(NE, P)
        Bt = take(2, NE * P)
        hid1 = arena[:, 0:KF * SEQ].rearrange("p (k t) -> p k t", k=KF)
        assert KF * SEQ <= at[0]
        xpad = take(12, SEQ + CONV - 1)
        qkv = take(12, SEQ)
        zs = take(HEADS, SEQ)
        spad = take(HEADS, SEQ + SC_CONV - 1)
        gc = take(HEADS, SEQ)
        gb = take(HEADS, SEQ)
        ysc = take(HEADS, SEQ)
        qkT = take(NE, P)
        M = take(NE, P)
        MT = take(NE, P)
        Y = take(NE, P)
        u0 = take(HEADS, P)
        vnew = take(HEADS, P)
        S1 = take(HEADS, P)
        nw = take(HEADS, P)
        kbg = take(HEADS, P)
        kdec = take(HEADS, P)
        qdec = take(HEADS, P)
        odn = take(HEADS, SEQ)
        gs1 = take(2, SEQ)
        ba_rows = gs1[0:NE, 0, :]
        cols = take(9, NE)
        beta, gin, gabs, gexp, gsp, gmax, glog, gcol, egc = (cols[:, i, :] for i in range(9))
        bge = take(1, NE)[:, 0, :]

        at[0] = 0
        qk = take(10, TOK)
        vt2 = take(4, KV_HEADS * P)
        prob = take(2, TOK)
        probT = take(2, TOK)
        vT = prob
        ksq = flat(probT).rearrange("p (a b) -> p a b", b=TOK)
        rope = flat(probT).rearrange("p (a b) -> p a b", b=SEQ)
        GATES = 3
        sg = take(GATES, TOK)
        lo = at[0]
        cbuf = take(KD, 2, SEQ + 2 * CPAD)
        co = take(KD, TOK)
        pbuf = take(KD, 2, SEQ + 2 * PPAD)
        hid2 = arena[:, lo:lo + KF * TOK].rearrange("p (k t) -> p k t", k=KF)
        assert KF * TOK <= at[0] - lo
        pooled = take(KD, TOK)
        ptmp = take(2, 2, SEQ + 2 * PPAD)
        abuf = flat(pooled)[:, 0:2 * 2 * (SEQ + 2)].rearrange("p (a b c) -> p a b c", a=2, b=2)
        stat = small[:, 84:108].rearrange("p (a b) -> p a b", b=4)
        bmod = small[:, 108:124].rearrange("p (k c) -> p k c", c=2)

        loaded = sem("x_and_tables_loaded")
        cond_loaded, vec2_loaded = sem("cond_loaded"), sem("vec2_loaded")
        vec1_loaded, ctx_loaded = sem("vec1_loaded"), sem("ctx_loaded")
        panel_loaded = [sem(f"panel_loaded{s}") for s in range(SLOTS)]
        panels_done = sem("panels_done")
        drained = [sem(f"drained{b}") for b in range(BANKS)]
        act_order, dve_order, pool_order = sem("act_order"), sem("dve_order"), sem("pool_order")
        squares_ready, sums_ready, root_ready, scale_ready, spread_ready = (
            sem(n) for n in ("squares_ready", "sums_ready", "root_ready", "scale_ready", "spread_ready"))
        h_ready, cond_ready, mods_ready = sem("h_ready"), sem("cond_ready"), sem("mods_ready")
        ba_out, ba_turned = sem("ba_out"), sem("ba_turned")
        ada_out, ada_turned = sem("ada_out"), sem("ada_turned")
        beta_ready, gin_ready, log_ready, g_ready = sem("beta_ready"), sem("gin_ready"), sem("log_ready"), sem("g_ready")
        conv1_ready, silu_ready = sem("conv1_ready"), sem("silu_ready")
        qk_ready, turned, ktok_ready, vtok_ready = sem("qk_ready"), sem("turned"), sem("ktok_ready"), sem("vtok_ready")
        cum_ready, diff_ready, decay_ready, exps_ready, kk_ready, kk_used, at_ready = (
            sem(n) for n in ("cum_ready", "diff_ready", "decay_ready", "exps_ready", "kk_ready", "kk_used", "at_ready"))
        blocks_ready, inv_mm, inv_turned, inv_y, inv_m = (
            sem(n) for n in ("blocks_ready", "inv_mm", "inv_turned", "inv_y", "inv_m"))
        keys_ready, scan_mm, scan_in = sem("keys_ready"), sem("scan_mm"), sem("scan_in")
        y_ready, mix_ready, stored, layer_opened = sem("y_ready"), sem("mix_ready"), sem("stored"), sem("layer_opened")

        block = ctx.enter_context(nc.Block())


        def done(l, j):
            return l * P1_ALL + (SLOTS + j + 1)

        def out_of(l, c):
            return l * (C1_ALL // BANKS) + (c // BANKS + 2)

        def done2(L, j):
            return P2_AT + L * P2_ALL + SLOTS + j + 1

        def out_of2(L, c):
            return (C2_AT + L * C2_ALL + c) // BANKS + 2

        def rows(w, k0=0, n=KD):
            return w.rearrange("(k p) n -> p k n", p=P)[:, k0:k0 + n, :]

        h2_ready, x2_ready, pads_ready = sem("h2_ready"), sem("x2_ready"), sem("pads_ready")
        rotated, perm_ready, rope_done = sem("rotated"), sem("perm_ready"), sem("rope_done")
        score_mm, max_ready, exp_ready, prob_ready = (sem(n) for n in ("score_mm", "max_ready", "exp_ready", "prob_ready"))
        turn_mm, probT_ready, o_mm, attn_ready = (sem(n) for n in ("turn_mm", "probT_ready", "o_mm", "attn_ready"))
        v_turned, v_ready, pooled_ready, gated = sem("v_turned"), sem("v_ready"), sem("pooled_ready"), sem("gated")
        total_ready, centred, lnorm_ready, lsilu_ready = sem("total_ready"), sem("centred"), sem("lnorm_ready"), sem("lsilu_ready")
        pairs_ready = sem("pairs_ready")
        aconv_ready, asilu_ready = sem("aconv_ready"), sem("asilu_ready")

        def width(L):
            return TOK if L == 0 else SEQ

        def streams(v, L):
            return v.rearrange("p (s t) -> p s t", t=SEQ)

        def mod(L, m, k, s):
            a = ((L * N_MOD + m) * KD + k) * 2 + s
            return mods[:, a:a + 1]

        def qk_tiles(L):
            return [(c, t) for c in range(10) for t in range(width(L) // P if c < N_HEADS else TOK // P)]

        def items(L):
            return [(h, t, 0 if t < 2 else SEQ, TOK if t < 2 else CTX) for h in range(N_HEADS) for t in range(width(L) // P)]

        def items_before(L):
            return sum(len(items(n)) for n in range(L))

        O_BANKS = (3, 7)
        SUM2 = DEPTH * N1_ALL + 1
        S_QK, S_CONV, S_LN1, S_LN2, S_ALL = 0, 1, 3, 5, 7
        R_QK, R_CONV, R_LN1, R_LN2, R_ALL = 0, 1, 2, 3, 4
        SQ2, SQ_ALL = 8 * DEPTH + 2, 14
        SP2, SP_ALL = 6 * DEPTH + 1, 16

        PAIRS = KD // 2
        total = pooled[:, 5, :]

        def load_second(sp, load):
            for L in range(DEPTH):
                wi = rows(w_in2[L])
                at_ = P2_AT + L * P2_ALL

                def put(j, src):
                    load(at_ + j, at_ + j, src)

                def four(j, first):
                    for n in range(4):
                        put(j + n, wi[:, :, first + n * PC:first + (n + 1) * PC])

                for j in range(4):
                    for n, first in enumerate((CONV_AT, GATE_AT)):
                        put(P2_CONV + 2 * j + n, wi[:, :, first + j * PC:first + (j + 1) * PC])
                for j in range(6):
                    put(P2_QKV + j, wi[:, :, Q_AT + j * PC:Q_AT + (j + 1) * PC])
                four(P2_POOL, POOL_AT)
                four(P2_G0, MIX_AT)
                for j in range(4):
                    put(P2_PMIX + j, rows(w_pool[L, j], 0, 2))
                four(P2_G2, MIX_AT + 2 * D)
                for j in range(4):
                    put(P2_PW + j, rows(w_pw[L])[:, :, j * PC:(j + 1) * PC])
                four(P2_G1, MIX_AT + D)
                for j in range(4):
                    put(P2_OUT + j, rows(w_out2[L])[:, :, j * PC:(j + 1) * PC])
                wu, wd = rows(w_up2[L]), w_down2[L]
                with sp.Fori(0, 3) as i:
                    for j in range(6):
                        load(6 * i + (at_ + P2_FFN + j), at_ + P2_FFN + j,
                             wu[:, :, bass.ds(3 * i * PC + (j % 2 * D_FF + j // 2 * PC), PC)])
                for j in range(18, 22):
                    first = j % 2 * D_FF + j // 2 * PC
                    put(P2_FFN + j, wu[:, :, first:first + PC])
                with sp.Fori(0, 2) as i:
                    for j in range(6):
                        load(6 * i + (at_ + P2_DOWN + j), at_ + P2_DOWN + j,
                             rows(wd, *KPARTS[j % 3])[:, :, bass.ds((2 * i + j // 3) * PC, PC)])
            sp.wait_ge(x2_ready, 1)

        def pool_second(pool):
            order = Order(pool, pool_order)
            pool.wait_ge(sums_ready, N_FINAL + 1)
            pool.dma_start(X[:, :, SEQ:TOK], ctx_in).then_inc(ctx_loaded, 16)
            for L in range(DEPTH):
                S = width(L) // SEQ
                pool.wait_ge(drained[3], out_of2(L, -1))
                for buf, pad in ((cbuf, CPAD), (pbuf, PPAD)):
                    for a in (0, pad + SEQ):
                        pool.memset(buf[:, :, :, a:a + pad], 0.0).then_inc(pads_ready, 1)
                pool.wait_ge(pads_ready, 4 * L + 4)
                pool.wait_ge(sums_ready, SUM2 + S_ALL * L + S_QK + 1)
                for c in range(KD):
                    g = c // 2
                    pool.wait_ge(drained[c % BANKS], out_of2(L, C2_POOL + c))
                    w, size = pbuf[:, c, 0:S, :], 1
                    for n in range(g + 1):
                        keep = SEQ + 2 * PPAD - 2 * size + 1
                        dst = ptmp[:, n % 2, 0:S, 0:keep]
                        order(pool.tensor_tensor(dst, w[:, :, 0:keep], w[:, :, size:size + keep], ALU.add))
                        order.wait()
                        w, size = dst, 2 * size
                    a = PPAD - size // 2
                    dst = streams(pooled[:, c, 0:S * SEQ], L)
                    order(pool.tensor_tensor(dst, w[:, :, a:a + SEQ], T("cnt", g * SEQ, SEQ).unsqueeze(1).to_broadcast([P, S, SEQ]), ALU.mult))
                    order.wait()
                    pool.tensor_tensor(dst, dst, pbuf[:, c, 0:S, PPAD:PPAD + SEQ], ALU.subtract).then_inc(pooled_ready, 1)

        def act_second(act, order, squares, root):
            def chunk(L, j, c, n):
                act.wait_ge(panels_done, done2(L, j))
                return ps[:, c % BANKS, 0:n]

            for L in range(DEPTH):
                n_tok = width(L)
                S = n_tok // SEQ
                for j in range(4):
                    for c in range(2):
                        src = chunk(L, P2_CONV + 2 * j + 1, 2 + c, n_tok)
                        if j:
                            act.wait_ge(drained[c], out_of2(L, C2_CONV + 4 * (j - 1) + c))
                        act.activation(sg[:, c, 0:n_tok], src, ACT.Sigmoid, bias=v2(L, "bin", 20 + 2 * j + c)).then_inc(drained[2 + c], 1)
                for c in range(12):
                    n = n_tok if c < N_HEADS else TOK
                    dst = qk[:, c, 0:n] if c < 10 else vT[:, c - 10, 0:n]
                    act.activation(dst, chunk(L, P2_QKV + c // 2, c, n), ACT.Identity, bias=v2(L, "bin", c)).then_inc(drained[c % BANKS], 1)
                act.wait_ge(drained[1], out_of2(L, C2_QKV + 9))
                squares(pooled[:, :, 0:n_tok], qk[:, 0:N_HEADS, 0:n_tok])
                squares(ksq, qk[:, N_HEADS:10, :])
                act.wait_ge(pads_ready, 4 * L + 4)
                for c in range(KD):
                    src = streams(chunk(L, P2_POOL + c // 2, c, n_tok), L)
                    act.activation(pbuf[:, c, 0:S, PPAD:PPAD + SEQ], src, ACT.Identity, bias=v2(L, "bin", 28 + c)).then_inc(drained[c % BANKS], 1)
                act.wait_ge(v_turned, L + 1)
                act.activation(flat(vt2), flat(ps[:, 4:6, :]), ACT.Copy).then_inc(v_ready, 1)
                root([SUM2 + S_ALL * L + S_QK], len(qk_tiles(L)))
                todo, a0 = items(L), items_before(L)

                def exp(i):
                    act.wait_ge(max_ready, a0 + i + 1)
                    if i >= 2:
                        act.wait_ge(turn_mm, a0 + i - 1)
                    n = todo[i][3]
                    act.activation(prob[:, i % 2, 0:n], ps[:, 4 + i % 2, 0:n], ACT.Exp, bias=stat[:, 1, i % 4:i % 4 + 1], scale=ATTN_SCALE,
                                   accum_out=stat[:, 2, i % 4:i % 4 + 1]).then_inc(exp_ready, 1)

                def output(i):
                    h, t, _, _ = todo[i]
                    act.wait_ge(o_mm, a0 + i + 1)
                    act.activation(qk[:, h, t * P:(t + 1) * P], ps[:, O_BANKS[i % 2], 0:P], ACT.Copy).then_inc(attn_ready, 1)

                exp(0)
                for i in range(len(todo)):
                    if i + 1 < len(todo):
                        exp(i + 1)
                    act.wait_ge(turn_mm, a0 + i + 1)
                    if i >= 2:
                        act.wait_ge(o_mm, a0 + i - 1)
                    n = todo[i][3]
                    act.activation(probT[:, i % 2, 0:n], ps[:, 6, 0:n], ACT.Copy).then_inc(probT_ready, 1)
                    if i:
                        output(i - 1)
                output(len(todo) - 1)

                def gates(j, c0, first, nth):
                    for c in range(KD):
                        src = chunk(L, j + c // 2, c0 + c, n_tok)
                        g = 24 * L + KD * nth + c
                        if g >= GATES:
                            act.wait_ge(gated, g - GATES + 1)
                        act.activation(sg[:, g % GATES, 0:n_tok], src, ACT.Sigmoid, bias=v2(L, "bin", first + c)).then_inc(drained[c % BANKS], 1)

                gates(P2_G0, C2_G0, 36, 0)
                for c in range(KD):
                    src = streams(chunk(L, P2_PMIX + c // 2, c, n_tok), L)
                    act.activation(pbuf[:, c, 0:S, PPAD:PPAD + SEQ], src, ACT.Copy, scale=v2(L, "psc", c)).then_inc(drained[c % BANKS], 1)
                gates(P2_G2, C2_G2, 52, 1)

                def variance(nth, s_at, src):
                    for k in range(PAIRS):
                        act.wait_ge(centred, (3 * L + nth) * PAIRS + k + 1)
                        squares(pooled[:, 2 * k:2 * k + 2, 0:n_tok], src[:, 2 * k:2 * k + 2, 0:n_tok])
                    root([SUM2 + S_ALL * L + s_at + 1], n_tok // P, "ln_eps")

                variance(0, S_CONV, co)
                for c in range(KD):
                    act.wait_ge(lnorm_ready, KD * L + c + 1)
                    act.activation(co[:, c, 0:n_tok], co[:, c, 0:n_tok], ACT.Silu, scale=v2(L, "clg", c), bias=v2(L, "clb", c)).then_inc(lsilu_ready, 1)
                for c in range(KD):
                    src = streams(chunk(L, P2_PW + c // 2, c, n_tok), L)
                    act.activation(cbuf[:, c, 0:S, CPAD:CPAD + SEQ], src, ACT.Identity, bias=v2(L, "pwb", c)).then_inc(drained[c % BANKS], 1)
                gates(P2_G1, C2_G1, 44, 2)
                variance(1, S_LN1, X)
                with act.Fori(0, KF // 2) as i:
                    for c in range(2):
                        act.wait_ge(panels_done, 2 * i + done2(L, P2_FFN))
                        act.wait_ge(aconv_ready, 2 * i + (2 * (KF // 2) * L + 2))
                        act.activation(abuf[:, c, 0:S, 1:1 + SEQ], streams(ps[:, c, 0:n_tok], L), ACT.Copy).then_inc(drained[c], 1)
                    for c in range(2):
                        act.wait_ge(aconv_ready, 2 * i + (2 * (KF // 2) * L + 2 + c + 1))
                        act.activation(sg[:, c, 0:n_tok], sg[:, c, 0:n_tok], ACT.Silu).then_inc(asilu_ready, 1)
                variance(2, S_LN2, X)

        def dve_second(dve, order, invert):
            def chunk(L, j, c, n):
                dve.wait_ge(panels_done, done2(L, j))
                return ps[:, c % BANKS, 0:n]

            dve.sem_inc(aconv_ready, 2)
            for L in range(DEPTH):
                n_tok = width(L)
                S = n_tok // SEQ
                tiles = n_tok // P
                lo_, hi_ = (lambda s: s * SEQ), (lambda s: (s + 1) * SEQ)
                if L == 0:
                    dve.wait_ge(h_ready, 16 * DEPTH + 8)
                    dve.wait_ge(mods_ready, DEPTH)
                    dve.wait_ge(ctx_loaded, 16)
                for m in (1, 4):
                    a = (L * N_MOD + m) * KD * 2
                    order(dve.tensor_scalar(mods[:, a:a + 2 * KD], mods[:, a:a + 2 * KD], 1.0, None, ALU.add))
                a = (L * N_MOD + 2) * KD * 2
                order(dve.tensor_tensor(bmod, mods[:, a:a + 2 * KD].rearrange("p (k c) -> p k c", c=2),
                                        v2(L, "bout", 0, KD).unsqueeze(2).to_broadcast([P, KD, 2]), ALU.mult))
                order.wait()

                def modulate(n_streams, m, step=None):
                    for k in range(KD):
                        if step:
                            order.wait(step(k))
                        for s in range(n_streams):
                            ins = dve.tensor_scalar(Hn[:, k, lo_(s):hi_(s)], X[:, k, lo_(s):hi_(s)], mod(L, m + 1, k, s), mod(L, m, k, s),
                                                    ALU.mult, ALU.add)
                        ins.then_inc(h2_ready, 1)

                modulate(2, 0, step if L else None)
                dve.wait_ge(h2_ready, 2 * KD * L + KD)
                for k in range(KD):
                    for s in range(S):
                        order(dve.tensor_scalar(X[:, k, lo_(s):hi_(s)], X[:, k, lo_(s):hi_(s)], ALPHA, bmod[:, k, s:s + 1], ALU.mult, ALU.add))
                for j in range(4):
                    for c in range(2):
                        dve.wait_ge(drained[2 + c], out_of2(L, C2_CONV + 4 * j + 2 + c))
                        k = 2 * j + c
                        dve.scalar_tensor_tensor(out=cbuf[:, k, 0:S, CPAD:CPAD + SEQ], in0=streams(ps[:, c, 0:n_tok], L), scalar=v2(L, "bin", 12 + k),
                                                 in1=streams(sg[:, c, 0:n_tok], L), op0=ALU.add, op1=ALU.mult).then_inc(drained[c], 1)
                dve.wait_ge(drained[1], out_of2(L, C2_CONV + 13))
                dve.wait_ge(pads_ready, 4 * L + 4)

                def depthwise(first, end):
                    with dve.Fori(first, end) as i:
                        order.enter(i, 2 * CW, first)
                        for j in range(CW):
                            for c in range(2):
                                src = cbuf[:, bass.ds(2 * i + c, 1), 0:S, j:j + SEQ].rearrange("p a s t -> p (a s) t")
                                acc = streams(flat(co[:, bass.ds(2 * i + c, 1), 0:n_tok]), L)
                                w = v2(L, "cw", 2 * i + (j * KD + c))
                                if j == 0:
                                    order(dve.tensor_scalar(acc, src, w, v2(L, "cb", 2 * i + c), ALU.mult, ALU.add))
                                else:
                                    order(dve.scalar_tensor_tensor(out=acc, in0=src, scalar=w, in1=acc, op0=ALU.mult, op1=ALU.add))
                            order.wait()
                        order.leave(end - first)

                depthwise(0, 3)
                invert([SUM2 + R_ALL * L + R_QK], len(qk_tiles(L)))
                for c in range(10):
                    n = n_tok if c < N_HEADS else TOK
                    b = 4 + c % 3
                    dve.wait_ge(spread_ready, SP2 + SP_ALL * L + c + 1)
                    dve.scalar_tensor_tensor(out=qk[:, c, 0:n], in0=qk[:, c, 0:n], scalar=v2(L, "qg" if c < N_HEADS else "kg"),
                                             in1=ps[:, b, 0:n], op0=ALU.mult, op1=ALU.mult).then_inc(rotated, 1)
                    dve.wait_ge(rotated, 10 * L + c + 1)
                    order(dve.tensor_tensor(rope[:, 0, :], qk[:, c, 0:SEQ], T("cos"), ALU.mult))
                    dve.wait_ge(perm_ready, 10 * L + c + 1)
                    order(dve.tensor_tensor(rope[:, 1, :], ps[:, b, 0:SEQ], T("sin"), ALU.mult))
                    order.wait()
                    dve.tensor_tensor(qk[:, c, 0:SEQ], rope[:, 0, :], rope[:, 1, :], ALU.add).then_inc(rope_done, 1)
                    dve.wait_ge(rope_done, 10 * L + c + 1)
                todo, a0 = items(L), items_before(L)

                def maximum(i):
                    s, n = i % 4, todo[i][3]
                    dve.wait_ge(score_mm, a0 + i + 1)
                    order(dve.tensor_reduce(stat[:, 0, s:s + 1], ps[:, 4 + i % 2, 0:n], AX.X, ALU.max))
                    order.wait()
                    dve.tensor_scalar(stat[:, 1, s:s + 1], stat[:, 0, s:s + 1], -ATTN_SCALE, None, ALU.mult).then_inc(max_ready, 1)

                maximum(0)
                for i in range(len(todo)):
                    if i + 1 < len(todo):
                        maximum(i + 1)
                    s, n = i % 4, todo[i][3]
                    dve.wait_ge(exp_ready, a0 + i + 1)
                    order(dve.reciprocal(stat[:, 3, s:s + 1], stat[:, 2, s:s + 1]))
                    order.wait()
                    dve.tensor_scalar(prob[:, i % 2, 0:n], prob[:, i % 2, 0:n], stat[:, 3, s:s + 1], None, ALU.mult).then_inc(prob_ready, 1)
                dve.wait_ge(attn_ready, a0 + len(todo))
                for c in range(KD):
                    g = 24 * L + c
                    dve.wait_ge(drained[c % BANKS], out_of2(L, C2_G0 + c))
                    dve.tensor_tensor(qk[:, c, 0:n_tok], qk[:, c, 0:n_tok], sg[:, g % GATES, 0:n_tok], ALU.mult).then_inc(gated, 1)

                def add_branch(nth, c0, branch):
                    for c in range(KD):
                        g = 24 * L + KD * nth + c
                        dve.wait_ge(drained[c % BANKS], out_of2(L, c0 + c))
                        v = streams(sg[:, g % GATES, 0:n_tok], L)
                        order(dve.tensor_tensor(v, v, branch(c), ALU.mult))
                        order.wait()
                        if g >= KD:
                            dve.wait_ge(gated, g - KD + 1)
                        dve.tensor_tensor(qk[:, c, 0:n_tok], qk[:, c, 0:n_tok], sg[:, g % GATES, 0:n_tok], ALU.add).then_inc(gated, 1)

                depthwise(3, 4)
                dve.wait_ge(panels_done, done2(L, P2_PMIX + 3))
                for k in range(1, KD):
                    ins = dve.tensor_tensor(total[:, 0:n_tok], total[:, 0:n_tok] if k > 1 else co[:, 0, 0:n_tok], co[:, k, 0:n_tok], ALU.add)
                    if k < KD - 1:
                        order(ins)
                        order.wait()
                    else:
                        ins.then_inc(total_ready, 1)
                add_branch(1, C2_G2, lambda c: pbuf[:, c, 0:S, PPAD:PPAD + SEQ])

                def centre(nth, s_at, sp_at, src):
                    dve.wait_ge(sums_ready, SUM2 + S_ALL * L + s_at + 1)
                    dve.tensor_copy(scales[:, 0:tiles], ps[:, 7, 0:tiles]).then_inc(scale_ready, 1)
                    dve.wait_ge(spread_ready, SP2 + SP_ALL * L + sp_at + 1)
                    for k in range(PAIRS + 1):
                        if k < PAIRS:
                            for c in (2 * k, 2 * k + 1):
                                ins = dve.tensor_tensor(src[:, c, 0:n_tok], src[:, c, 0:n_tok], ps[:, 4, 0:n_tok], ALU.subtract)
                            ins.then_inc(centred, 1)
                        if k:
                            v = pooled[:, 2 * k - 2:2 * k, 0:n_tok]
                            dve.wait_ge(squares_ready, SQ2 + SQ_ALL * L + 2 + PAIRS * nth + k)
                            dve.tensor_tensor(v[:, 0, :], v[:, 0, :], v[:, 1, :], ALU.add).then_inc(pairs_ready, 1)
                    dve.wait_ge(centred, (3 * L + nth + 1) * PAIRS)
                    invert([SUM2 + R_ALL * L + R_CONV + nth], tiles)
                    dve.wait_ge(spread_ready, SP2 + SP_ALL * L + sp_at + 2)

                def layer_norm(nth, s_at, sp_at, gain, bias):
                    centre(nth, s_at, sp_at, X)
                    scaled, last = [], []
                    for k in range(KD + 1):
                        if k < KD:
                            scaled.append(order(dve.tensor_tensor(X[:, k, 0:n_tok], X[:, k, 0:n_tok], ps[:, 5, 0:n_tok], ALU.mult)))
                        if k:
                            order.wait(scaled[k - 1])
                            last.append(order(dve.tensor_scalar(X[:, k - 1, 0:n_tok], X[:, k - 1, 0:n_tok], v2(L, gain, k - 1), v2(L, bias, k - 1),
                                                                ALU.mult, ALU.add)))
                    return lambda k: last[k]

                def add_gated(j, step, c0, m):
                    for c in range(KD + 1):
                        if c < KD:
                            v = chunk(L, j + c // 2 * step, c0 + c, n_tok)
                            for s in range(S):
                                ins = dve.scalar_tensor_tensor(out=X[:, c, lo_(s):hi_(s)], in0=v[:, lo_(s):hi_(s)], scalar=mod(L, m, c, s),
                                                               in1=X[:, c, lo_(s):hi_(s)], op0=ALU.mult, op1=ALU.add)
                            ins.then_inc(drained[c % BANKS], 1)
                        if c >= 2:
                            for k in (c - 2, c - 1):
                                dve.wait_ge(drained[k % BANKS], out_of2(L, c0 + k))
                            if c > 2:
                                order.wait()
                            ins = dve.tensor_tensor(total[:, 0:n_tok], total[:, 0:n_tok] if c > 2 else X[:, 0, 0:n_tok], X[:, c - 1, 0:n_tok], ALU.add)
                            if c < KD:
                                order(ins)
                            else:
                                ins.then_inc(total_ready, 1)

                centre(0, S_CONV, 10, co)
                for k in range(KD):
                    dve.tensor_tensor(co[:, k, 0:n_tok], co[:, k, 0:n_tok], ps[:, 5, 0:n_tok], ALU.mult).then_inc(lnorm_ready, 1)
                add_branch(2, C2_G1, lambda c: cbuf[:, c, 0:S, CPAD:CPAD + SEQ])
                add_gated(P2_OUT, 1, C2_OUT, 2)
                step = layer_norm(1, S_LN1, 12, "l1g", "l1b")
                modulate(S, 3, step)
                order(dve.memset(abuf[:, :, :, 0:1], 0.0))
                order(dve.memset(abuf[:, :, :, 1 + SEQ:2 + SEQ], 0.0))
                dve.wait_ge(h2_ready, 2 * KD * L + 2 * KD)
                order(dve.tensor_scalar(X[:, :, 0:n_tok], X[:, :, 0:n_tok], ALPHA, None, ALU.mult))
                order.wait()
                with dve.Fori(0, KF // 2) as i:
                    order.enter(i, 4)
                    for j in range(3):
                        for c in range(2):
                            src, acc = abuf[:, c, 0:S, j:j + SEQ], streams(sg[:, c, 0:n_tok], L)
                            w = v2(L, "fw", 2 * i + (j * KF + c))
                            if j == 0:
                                dve.wait_ge(drained[c], i + out_of2(L, C2_FFN + c))
                                dve.wait_ge(drained[2 + c], i + out_of2(L, C2_FFN - BANKS + 2 + c))
                                order(dve.tensor_scalar(acc, src, w, v2(L, "fb", 2 * i + c), ALU.mult, ALU.add))
                            else:
                                ins = dve.scalar_tensor_tensor(out=acc, in0=src, scalar=w, in1=acc, op0=ALU.mult, op1=ALU.add)
                                if j == 1:
                                    order(ins)
                                else:
                                    ins.then_inc(aconv_ready, 1)
                        if j < 2:
                            order.wait()
                    for c in range(2):
                        dve.wait_ge(asilu_ready, 2 * i + (2 * (KF // 2) * L + c + 1))
                        dve.wait_ge(panels_done, 2 * i + done2(L, P2_FFN + 1))
                        dve.tensor_tensor(flat(hid2[:, bass.ds(2 * i + c, 1), 0:n_tok]), sg[:, c, 0:n_tok], ps[:, 2 + c, 0:n_tok],
                                          ALU.mult).then_inc(drained[2 + c], 1)
                    order.leave(KF // 2)
                add_gated(P2_DOWN + 2, 3, C2_DOWN, 5)
                step = layer_norm(2, S_LN2, 14, "l2g", "l2b")
                if L == DEPTH - 1:
                    order.wait()
                    dve.sem_inc(x2_ready, 1)

        def pe_second(pe, sums, spread, panel):
            for L in range(DEPTH):
                n_tok = width(L)
                tiles = n_tok // P
                a_p = P2_AT + L * P2_ALL

                def panel2(j, c, rhs, n=n_tok, turn=0, turn_c=0, **more):
                    panel(a_p + j, turn * (16 * (6 // SLOTS)) + 16 * ((a_p + j) // SLOTS + 1), [turn_c + out_of2(L, c + m - BANKS) for m in range(2)], c,
                          lambda k: rhs[:, k, 0:n], n, **more)

                def four(j, c, rhs):
                    for m in range(4):
                        panel2(j + m, c + 2 * m, rhs)

                def layer_norm(s_at, nth):
                    pe.wait_ge(total_ready, 3 * L + nth + 1)
                    sums([[total[:, t * P:(t + 1) * P]] for t in range(tiles)], T("inv_d"))
                    pe.wait_ge(scale_ready, SUM2 + S_ALL * L + s_at + 1)
                    spread(4, 0, tiles)
                    for k in range(PAIRS):
                        pe.wait_ge(pairs_ready, (3 * L + nth) * PAIRS + k + 1)
                        for t in range(tiles):
                            last = pe.matmul(ps[:, 7, t:t + 1], pooled[:, 2 * k, t * P:(t + 1) * P], T("inv_d"),
                                             start=(k == 0 and t == 0), stop=(k == PAIRS - 1 and t == tiles - 1))
                    last.then_inc(sums_ready, 1)
                    pe.wait_ge(scale_ready, SUM2 + S_ALL * L + s_at + 2)
                    spread(5, 0, tiles)

                for j in range(8):
                    panel2(P2_CONV + j, C2_CONV + 2 * j, Hn, ready=(h2_ready, 2 * KD * L) if j == 0 else None)
                pe.wait_ge(h2_ready, 2 * KD * L + KD)
                for j in range(6):
                    panel2(P2_QKV + j, C2_QKV + 2 * j, Hn, n_tok if j < 4 else TOK)
                four(P2_POOL, C2_POOL, Hn)
                pe.wait_ge(drained[3], out_of2(L, C2_QKV + 11))
                for t in range(4):
                    for v in range(KV_HEADS):
                        e = KV_HEADS * t + v
                        last = pe.transpose(ps[:, 4 + e // 4, e % 4 * P:(e % 4 + 1) * P], vT[:, v, t * P:(t + 1) * P], ident)
                last.then_inc(v_turned, 1)
                pe.wait_ge(squares_ready, SQ2 + SQ_ALL * L + 2)
                cells = qk_tiles(L)
                sums([[(pooled[:, c, :] if c < N_HEADS else ksq[:, c - N_HEADS, :])[:, t * P:(t + 1) * P]] for c, t in cells], T("inv_p"))
                pe.wait_ge(scale_ready, SUM2 + S_ALL * L + S_QK + 1)
                pe.wait_ge(v_ready, L + 1)

                def norm_spread(c):
                    spread(4 + c % 3, cells.index((c, 0)), sum(m == c for m, _ in cells))

                for c in range(3):
                    norm_spread(c)
                for c in range(10):
                    pe.wait_ge(rotated, 10 * L + c + 1)
                    pe.matmul(ps[:, 4 + c % 3, 0:SEQ], T("perm"), qk[:, c, 0:SEQ], start=True, stop=True).then_inc(perm_ready, 1)
                    if c + 3 < 10:
                        pe.wait_ge(rope_done, 10 * L + c + 1)
                        norm_spread(c + 3)
                pe.wait_ge(rope_done, 10 * L + 10)
                pe.wait_ge(drained[3], out_of2(L, C2_POOL + 7))
                todo, a0 = items(L), items_before(L)

                def score(i):
                    h, t, k0, n = todo[i]
                    if i >= 2:
                        pe.wait_ge(exp_ready, a0 + i - 1)
                    pe.matmul(ps[:, 4 + i % 2, 0:n], qk[:, h, t * P:(t + 1) * P], qk[:, N_HEADS + h // (N_HEADS // KV_HEADS), k0:k0 + n],
                              start=True, stop=True).then_inc(score_mm, 1)

                score(0)
                score(1)
                for i, (h, t, k0, n) in enumerate(todo):
                    kv = h // (N_HEADS // KV_HEADS)
                    pe.wait_ge(prob_ready, a0 + i + 1)
                    if i:
                        pe.wait_ge(probT_ready, a0 + i)
                    for m in range(n // P):
                        last = pe.transpose(ps[:, 6, m * P:(m + 1) * P], prob[:, i % 2, m * P:(m + 1) * P], ident)
                    last.then_inc(turn_mm, 1)
                    if i + 2 < len(todo):
                        score(i + 2)
                    pe.wait_ge(probT_ready, a0 + i + 1)
                    if i >= 2:
                        pe.wait_ge(attn_ready, a0 + i - 1)
                    for m in range(n // P):
                        last = pe.matmul(ps[:, O_BANKS[i % 2], 0:P], vt2[:, k0 // P + m, kv * P:(kv + 1) * P], probT[:, i % 2, m * P:(m + 1) * P],
                                         start=(m == 0), stop=(m == n // P - 1))
                    last.then_inc(o_mm, 1)
                pe.wait_ge(attn_ready, a0 + len(todo))
                four(P2_G0, C2_G0, Hn)
                pe.wait_ge(pooled_ready, KD * (L + 1))
                for j in range(4):
                    panel2(P2_PMIX + j, C2_PMIX + 2 * j, pooled[:, 2 * j:2 * j + 2, :], part=(0, 2), k_all=2)
                four(P2_G2, C2_G2, Hn)
                layer_norm(S_CONV, 0)
                for m in range(4):
                    panel2(P2_PW + m, C2_PW + 2 * m, co, ready=(lsilu_ready, KD * L) if m == 0 else None)
                four(P2_G1, C2_G1, Hn)
                for m in range(4):
                    panel2(P2_OUT + m, C2_OUT + 2 * m, qk, ready=(gated, 24 * L + 16) if m == 0 else None)
                layer_norm(S_LN1, 1)
                with pe.Fori(0, 3) as i:
                    for j in range(6):
                        panel2(P2_FFN + j, C2_FFN + 2 * j, Hn, turn=i, turn_c=3 * i, ready=(h2_ready, 2 * KD * L + KD) if j == 0 else None)
                for j in range(18, 22):
                    panel2(P2_FFN + j, C2_FFN + 2 * j, Hn)
                with pe.Fori(0, 2) as i:
                    pe.wait_ge(drained[3], out_of2(L, C2_FFN + 43))
                    for j in range(6):
                        panel2(P2_DOWN + j, C2_DOWN + j // 3 * 2, hid2, turn=i, turn_c=i, part=KPARTS[j % 3], k_all=KF)
                layer_norm(S_LN2, 2)

        @block.sync
        def _(sp):
            sp.dma_start(X1, x).then_inc(loaded, 16)
            sp.dma_start(tab[:, :], tabs).then_inc(loaded, 16)
            sp.sem_inc(panels_done, SLOTS)
            for b in range(BANKS):
                sp.sem_inc(drained[b], 1)

            def load(panel, j, src, waited=False):
                s = j % SLOTS
                if not waited:
                    sp.wait_ge(panels_done, panel + 1)
                sp.dma_start(W[:, s, 0:src.shape[1], 0:src.shape[2]], src).then_inc(panel_loaded[s], 16)

            with sp.Fori(0, DEPTH) as l:
                at_ = l * P1_ALL
                wi = rows(w_in[l])
                for j in range(2):
                    load(at_ + (P1_BA + j), P1_BA + j, wi[:, 4 * j:4 * j + 4, B_AT:B_AT + NE])
                sp.wait_ge(panels_done, at_ + (P1_QKV + 1))
                sp.sem_inc(layer_opened, 1)
                load(at_ + P1_QKV, P1_QKV, wi[:, :, 0:PC], waited=True)
                for j in range(1, 8):
                    load(at_ + (P1_QKV + j), P1_QKV + j, wi[:, :, j * PC:(j + 1) * PC])
                for j, part in enumerate((1, 1, 2, 2, 0, 0)):
                    c = SC_AT + 512 * part + PC * (j % 2)
                    load(at_ + (P1_GC + j), P1_GC + j, wi[:, :, c:c + PC])
                with sp.Fori(0, 4) as i:
                    for j in range(6):
                        load(at_ + (P1_ADA + j) + 6 * i, P1_ADA + j, rows(w_ada[l])[:, :, bass.ds((6 * i + j) * PC, PC)])
                for j in range(4):
                    load(at_ + (P1_OUT + j), P1_OUT + j, rows(w_out[l])[:, :, j * PC:(j + 1) * PC])
                with sp.Fori(0, 3) as i:
                    for j in range(6):
                        w = rows((w_gate, w_up)[j % 2][l])
                        load(at_ + (P1_FFN + j) + 6 * i, P1_FFN + j, w[:, :, bass.ds((3 * i + j // 2) * PC, PC)])
                for j in range(18, 22):
                    w = rows((w_gate, w_up)[j % 2][l])
                    load(at_ + (P1_FFN + j), P1_FFN + j, w[:, :, j // 2 * PC:(j // 2 + 1) * PC])
                with sp.Fori(0, 2) as i:
                    for j in range(6):
                        w = rows(w_down[l], *KPARTS[j % 3])
                        load(at_ + (P1_DOWN + j) + 6 * i, P1_DOWN + j, w[:, :, bass.ds((2 * i + j // 3) * PC, PC)])
            load_second(sp, load)
            sp.dma_start(out, X1).then_inc(stored, 16)
            sp.wait_ge(stored, 16)

        @block.gpsimd
        def _(pool):
            pool.dma_start(cnd, cond).then_inc(cond_loaded, 16)
            pool.dma_start(pf[:, :], vec_final).then_inc(vec2_loaded, 16)
            pool.dma_start(p2[:, :], vec2).then_inc(vec2_loaded, 16)
            with pool.Fori(0, DEPTH) as l:
                pool.wait_ge(drained[3], out_of(l, -1))
                pool.dma_start(p1[:, :], vec1[l]).then_inc(vec1_loaded, 16)
                pool.wait_ge(at_ready, l + 1)
                for s in range(LEVELS):
                    if s >= 2:
                        pool.wait_ge(inv_m, l * LEVELS + (s - 1))
                    pool.tensor_tensor(Bt[:, s % 2, :].rearrange("p (e c) -> p e c", e=NE), AT,
                                       T("level", s * P, P).unsqueeze(1).to_broadcast([P, NE, P]),
                                       ALU.mult).then_inc(blocks_ready, 1)
            pool_second(pool)

        @block.scalar
        def _(act):
            order = Order(act, act_order)
            act.wait_ge(loaded, 32)

            def squares(dst, src):
                act.activation(dst, src, ACT.Square).then_inc(squares_ready, 1)

            def root(nth, n, eps="eps"):
                act.wait_ge(sums_ready, nth[0] + 1)
                act.activation(roots[:, 0:n], ps[:, 7, 0:n], ACT.Sqrt, bias=T(eps)).then_inc(root_ready, 1)

            def evacuate(l, j, c, dst, func=ACT.Copy):
                act.wait_ge(panels_done, done(l, j))
                act.activation(dst, ps[:, c % BANKS, 0:SEQ], func).then_inc(drained[c % BANKS], 1)

            def ada(l, jj):
                act.wait_ge(panels_done, done(l, P1_ADA + jj))
                if jj >= 12:
                    act.wait_ge(ada_turned, N_ADA * l + (jj - 11))
                act.activation(ada_rows(jj), ps[0:2, jj % ADA_BANKS, 0:PC], ACT.Copy).then_inc(ada_out, 1)

            act.wait_ge(cond_loaded, 16)
            act.activation(cnd, cnd, ACT.Silu).then_inc(cond_ready, 1)
            with act.Fori(0, DEPTH) as l:
                order.enter(l, 5)
                norm = l * N1_ALL
                act.wait_ge(drained[3], out_of(l, -1))
                for k in range(2):
                    squares(sq1[:, 4 * k:4 * k + 4, :], X1[:, 4 * k:4 * k + 4, :])
                root([norm + N1_IN], 2)
                act.wait_ge(vec1_loaded, 16 * l + 16)
                act.wait_ge(gin_ready, l + 1)
                act.activation(beta.rearrange("p (n h) -> p n h", n=2), ps[:, 6, 0:2 * NE].rearrange("p (n h) -> p n h", n=2)[:, :, 0:HEADS],
                               ACT.Sigmoid).then_inc(beta_ready, 1)
                order(act.activation(gabs, gin, ACT.Abs))
                order.wait()
                order(act.activation(gexp, gabs, ACT.Exp, scale=-1.0))
                order(act.activation(rates, v1("alog", 0, HEADS), ACT.Exp))
                order.wait()
                act.activation(gsp, gexp, ACT.Ln, bias=T("one")).then_inc(log_ready, 1)
                for c in range(14):
                    if c < 12:
                        evacuate(l, P1_QKV + c // 2, C1_QKV + c, xpad[:, c, CONV - 1:])
                    if c >= 2:
                        act.wait_ge(conv1_ready, 12 * l + (c - 1))
                        act.activation(qkv[:, c - 2, :], qkv[:, c - 2, :], ACT.Silu).then_inc(silu_ready, 1)
                for c in range(4):
                    evacuate(l, P1_Z + c // 2, C1_Z + c, zs[:, c, :], ACT.Silu)
                act.wait_ge(silu_ready, 12 * l + 8)
                for k in range(2):
                    squares(sq1[:, 4 * k:4 * k + 4, :], qkv[:, 4 * k:4 * k + 4, :])
                root([norm + N1_L2], 16)
                for c in range(4):
                    evacuate(l, P1_GC + c // 2, C1_GC + c, gc[:, c, :])
                act.wait_ge(turned, 2 * l + 1)
                act.activation(flat(ktok), flat(ps[:, 4:6, :]), ACT.Copy).then_inc(ktok_ready, 1)
                for c in range(4):
                    evacuate(l, P1_GB + c // 2, C1_GB + c, gb[:, c, :])
                act.wait_ge(diff_ready, l + 1)
                act.activation(flat(DT), flat(DT), ACT.Exp).then_inc(decay_ready, 1)
                act.activation(egc, gcol, ACT.Exp)
                act.activation(flat(qdec), ps[:, 5, :], ACT.Exp).then_inc(exps_ready, 1)
                for jj in range(7):
                    ada(l, jj)
                for s in range(1, LEVELS):
                    act.wait_ge(inv_mm, l * (2 * LEVELS - 1) + 2 * s)
                    act.activation(flat(Y), flat(ps[:, 4:6, :]), ACT.Copy).then_inc(inv_y, 1)
                    for jj in range(2):
                        ada(l, 5 + 2 * s + jj)
                act.wait_ge(scan_mm, 6 * l + 1)
                act.activation(flat(u0), ps[:, 4, :], ACT.Copy).then_inc(scan_in, 1)
                act.wait_ge(scan_mm, 6 * l + 2)
                act.activation(flat(nw), ps[:, 5, :], ACT.Copy, scale=-1.0).then_inc(scan_in, 1)
                ada(l, 19)
                act.wait_ge(scan_mm, 6 * l + 3)
                act.activation(flat(S1), ps[:, 6, :], ACT.Copy).then_inc(scan_in, 1)
                act.wait_ge(scan_mm, 6 * l + 4)
                order(act.activation(odn[:, :, 0:P], ps[:, 7, :].rearrange("p (h c) -> p h c", h=HEADS), ACT.Copy))
                ada(l, 20)
                act.wait_ge(scan_mm, 6 * l + 5)
                act.activation(flat(vnew), ps[:, 4, :], ACT.Copy).then_inc(scan_in, 1)
                ada(l, 21)
                act.wait_ge(scan_mm, 6 * l + 6)
                order(act.activation(odn[:, :, P:SEQ], ps[:, 5, :].rearrange("p (h c) -> p h c", h=HEADS), ACT.Copy))
                act.wait_ge(y_ready, HEADS * l + HEADS)
                squares(sq1[:, 4:8, :], ysc)
                order.wait()
                squares(sq1[:, 0:4, :], odn)
                for jj in range(22, N_ADA):
                    ada(l, jj)
                root([norm + N1_MIX], 16)
                act.wait_ge(drained[3], out_of(l, C1_OUT + 7))
                for k in range(2):
                    squares(sq1[:, 4 * k:4 * k + 4, :], X1[:, 4 * k:4 * k + 4, :])
                root([norm + N1_FFN], 2)
                with act.Fori(0, KF // 2) as i:
                    for c in range(2):
                        act.wait_ge(panels_done, done(l, P1_FFN) + 2 * i)
                        act.wait_ge(drained[2 + c], out_of(l, C1_FFN - BANKS + 2 + c) + i)
                        act.activation(gs1[:, c, :], ps[:, c, 0:SEQ], ACT.Silu).then_inc(drained[c], 1)
                order.leave(DEPTH)
            act.wait_ge(drained[3], out_of(DEPTH - 1, C1_DOWN + 7))
            for k in range(2):
                squares(sq1[:, 4 * k:4 * k + 4, :], X1[:, 4 * k:4 * k + 4, :])
            root([N_FINAL], 2)
            act.wait_ge(vec2_loaded, 32)
            act_second(act, order, squares, root)

        @block.vector
        def _(dve):
            order = Order(dve, dve_order)

            def invert(nth, n):
                dve.wait_ge(root_ready, nth[0] + 1)
                dve.reciprocal(scales[:, 0:n], roots[:, 0:n]).then_inc(scale_ready, 1)

            def chunk(l, j, c):
                dve.wait_ge(panels_done, done(l, j))
                return ps[:, c % BANKS, 0:SEQ]

            def normalise(norm, spreads, gain, dst):
                invert([norm], 2)
                dve.wait_ge(spread_ready, spreads)
                for k in range(KD):
                    dve.scalar_tensor_tensor(out=dst[:, k, :], in0=X1[:, k, :], scalar=gain(k), in1=ps[:, 4, 0:SEQ],
                                             op0=ALU.mult, op1=ALU.mult).then_inc(h_ready, 1)

            def tiles(v):
                return v.rearrange("p (n h) -> p n h", n=2)

            dve.memset(xpad[:, :, 0:CONV - 1], 0.0)
            dve.memset(spad[:, :, 0:SC_CONV - 1], 0.0)
            dve.wait_ge(loaded, 32)
            with dve.Fori(0, DEPTH) as l:
                order.enter(l, 67)
                norm = l * N1_ALL
                dve.wait_ge(vec1_loaded, 16 * l + 16)
                normalise(norm + N1_IN, l * 6 + 1, lambda k: v1("norm1", k), H1)
                dve.wait_ge(panels_done, done(l, P1_BA + 1))
                dve.tensor_copy(ba_rows, ps[0:NE, 5, 0:SEQ]).then_inc(ba_out, 1)
                dve.wait_ge(ba_turned, l + 1)
                dve.tensor_tensor(tiles(gin), tiles(ps[:, 6, 0:2 * NE])[:, :, HEADS:NE],
                                  v1("dtb", 0, HEADS).unsqueeze(1).to_broadcast([P, 2, HEADS]), ALU.add).then_inc(gin_ready, 1)
                dve.wait_ge(log_ready, l + 1)
                order(dve.scalar_tensor_tensor(out=gmax, in0=gin, scalar=0.0, in1=gsp, op0=ALU.max, op1=ALU.add))
                order.wait()
                dve.scalar_tensor_tensor(out=tiles(glog), in0=tiles(gmax), scalar=-1.0,
                                         in1=rates.unsqueeze(1).to_broadcast([P, 2, HEADS]),
                                         op0=ALU.mult, op1=ALU.mult).then_inc(g_ready, 1)
                for c0 in range(0, 12, 2):
                    for j in range(CONV):
                        for c in range(c0, c0 + 2):
                            w = v1("dnw", j * 12 + c)
                            src = xpad[:, c, j:j + SEQ]
                            if j == 0:
                                dve.wait_ge(drained[c % BANKS], out_of(l, C1_QKV + c))
                                order(dve.tensor_scalar(qkv[:, c, :], src, w, None, ALU.mult))
                            else:
                                ins = dve.scalar_tensor_tensor(out=qkv[:, c, :], in0=src, scalar=w, in1=qkv[:, c, :],
                                                               op0=ALU.mult, op1=ALU.add)
                                if j < CONV - 1:
                                    order(ins)
                                else:
                                    ins.then_inc(conv1_ready, 1)
                        if j < CONV - 1:
                            order.wait()
                invert([norm + N1_L2], 16)
                for i in range(2):
                    dve.wait_ge(spread_ready, l * 6 + 2 + i)
                    v = flat(qkv[:, 4 * i:4 * i + 4, :])
                    dve.scalar_tensor_tensor(out=v, in0=v, scalar=P ** -0.5 if i == 0 else 1.0, in1=flat(ps[:, 4 + 2 * i:6 + 2 * i, :]),
                                             op0=ALU.mult, op1=ALU.mult).then_inc(qk_ready, 1)
                for c in range(4):
                    dve.wait_ge(drained[c], out_of(l, C1_GC + c))
                    dve.tensor_tensor(spad[:, c, SC_CONV - 1:], chunk(l, P1_HV + c // 2, C1_HV + c), gc[:, c, :], ALU.mult).then_inc(drained[c], 1)
                dve.wait_ge(turned, 2 * l + 2)
                dve.wait_ge(beta_ready, l + 1)
                dve.tensor_tensor(vtok, flat(ps[:, 6:8, :]).rearrange("p (e c) -> p e c", e=NE),
                                  beta.unsqueeze(2).to_broadcast([P, NE, P]), ALU.mult).then_inc(vtok_ready, 1)
                dve.wait_ge(cum_ready, 2 * l + 1)
                order(dve.tensor_copy(gcol, ps[:, 6, 0:NE]))
                order.wait()
                dve.wait_ge(cum_ready, 2 * l + 2)
                for e in range(NE):
                    ins = dve.scalar_tensor_tensor(out=DT[:, e, :], in0=ps[:, 4 + e // 4, e % 4 * P:(e % 4 + 1) * P],
                                                   scalar=gcol[:, e:e + 1], in1=T("cap"), op0=ALU.subtract, op1=ALU.min)
                ins.then_inc(diff_ready, 1)
                dve.wait_ge(decay_ready, l + 1)
                dve.wait_ge(kk_ready, 3 * l + 1)
                dve.tensor_tensor(flat(AT), flat(ps[:, 6:8, :]), flat(DT), ALU.mult).then_inc(kk_used, 1)
                dve.wait_ge(kk_used, l + 1)
                dve.wait_ge(kk_ready, 3 * l + 2)
                dve.tensor_tensor(flat(AT), flat(ps[:, 4:6, :]), flat(AT), ALU.mult).then_inc(at_ready, 1)
                dve.wait_ge(kk_ready, 3 * l + 3)
                dve.tensor_tensor(flat(qkT), flat(ps[:, 6:8, :]), flat(DT), ALU.mult)
                dve.wait_ge(drained[3], out_of(l, C1_HV + 3))
                for j in range(SC_CONV):
                    for c in range(4):
                        w = v1("scw", j * 4 + c)
                        src = spad[:, c, j:j + SEQ]
                        if j == 0:
                            order(dve.tensor_scalar(ysc[:, c, :], src, w, None, ALU.mult))
                        else:
                            order(dve.scalar_tensor_tensor(out=ysc[:, c, :], in0=src, scalar=w, in1=ysc[:, c, :],
                                                           op0=ALU.mult, op1=ALU.add))
                    order.wait()
                for c in range(4):
                    dve.wait_ge(drained[c], out_of(l, C1_GB + c))
                    dve.tensor_tensor(ysc[:, c, :], ysc[:, c, :], gb[:, c, :], ALU.mult).then_inc(y_ready, 1)
                dve.wait_ge(blocks_ready, l * LEVELS + 1)
                dve.scalar_tensor_tensor(out=MT, in0=Bt[:, 0, :].rearrange("p (e c) -> p e c", e=NE), scalar=-1.0,
                                         in1=ident.unsqueeze(1).to_broadcast([P, NE, P]),
                                         op0=ALU.mult, op1=ALU.add).then_inc(inv_m, 1)
                dve.wait_ge(inv_mm, l * (2 * LEVELS - 1) + 1)
                dve.tensor_copy(flat(M), flat(ps[:, 4:6, :])).then_inc(inv_turned, 1)
                dve.wait_ge(exps_ready, l + 1)
                order(dve.tensor_tensor(bge, beta, egc, ALU.mult))
                order.wait()
                for h in range(HEADS):
                    order(dve.tensor_scalar(kbg[:, h, :], ktok[:, HEADS + h, :], bge[:, HEADS + h:HEADS + h + 1], None, ALU.mult))
                    order(dve.tensor_scalar(kdec[:, h, :], ktok[:, h, :], DT[:, h, P - 1:P], None, ALU.mult))
                dve.tensor_tensor(qdec, qdec, qkv[:, 0:HEADS, P:SEQ], ALU.mult).then_inc(keys_ready, 1)
                for s in range(1, LEVELS):
                    dve.wait_ge(inv_mm, l * (2 * LEVELS - 1) + (2 * s + 1))
                    if s < LEVELS - 1:
                        if s == 1:
                            dve.wait_ge(inv_turned, l + 1)
                        else:
                            dve.wait_ge(inv_m, l * LEVELS + s)
                        dve.tensor_tensor(flat(M), flat(M), flat(ps[:, 6:8, :]), ALU.subtract)
                    dve.tensor_tensor(flat(MT), flat(MT), flat(ps[:, 4:6, :]), ALU.subtract).then_inc(inv_m, 1)
                invert([norm + N1_MIX], 16)
                dve.wait_ge(ada_turned, N_ADA * l + N_ADA)
                dve.tensor_tensor(mods[:, bass.ds(l * (N_MOD * KD * 2), N_MOD * KD * 2)].rearrange("p (k c) -> p k c", c=2),
                                  ps[:, 3, 0:N_MOD * KD * 2].rearrange("p (k c) -> p k c", c=2),
                                  v1("ada", 0, N_MOD * KD).unsqueeze(2).to_broadcast([P, N_MOD * KD, 2]),
                                  ALU.add).then_inc(mods_ready, 1)
                for i in range(2):
                    dve.wait_ge(spread_ready, l * 6 + 4 + i)
                    for h in range(HEADS):
                        ins = dve.scalar_tensor_tensor(out=mix1[:, 4 * i + h, :], in0=(odn, ysc)[i][:, h, :],
                                                       scalar=v1("dng") if i == 0 else v1("scg", h),
                                                       in1=ps[:, 4 + 2 * i + h // 2, h % 2 * SEQ:(h % 2 + 1) * SEQ],
                                                       op0=ALU.mult, op1=ALU.mult)
                        order(ins)
                order.wait()
                dve.wait_ge(drained[3], out_of(l, C1_Z + 3))
                dve.tensor_tensor(mix1[:, 0:4, :], mix1[:, 0:4, :], zs, ALU.mult).then_inc(mix_ready, 1)
                for c in range(KD):
                    v = chunk(l, P1_OUT + c // 2, C1_OUT + c)
                    dve.tensor_tensor(X1[:, c, :], X1[:, c, :], v, ALU.add).then_inc(drained[c % BANKS], 1)
                normalise(norm + N1_FFN, l * 6 + 6, lambda k: v1("norm2", k), H1)
                with dve.Fori(0, KF // 2) as i:
                    for c in range(2):
                        dve.wait_ge(drained[c], out_of(l, C1_FFN + c) + i)
                        dve.wait_ge(panels_done, done(l, P1_FFN + 1) + 2 * i)
                        dve.tensor_tensor(hid1[:, bass.ds(2 * i + c, 1), :].rearrange("p a t -> p (a t)"), gs1[:, c, :],
                                          ps[:, 2 + c, 0:SEQ], ALU.mult).then_inc(drained[2 + c], 1)
                for c in range(KD):
                    v = chunk(l, P1_DOWN + 2 + c // 2 * 3, C1_DOWN + c)
                    dve.tensor_tensor(X1[:, c, :], X1[:, c, :], v, ALU.add).then_inc(drained[c % BANKS], 1)
                order.leave(DEPTH)
            dve.wait_ge(vec2_loaded, 32)
            normalise(N_FINAL, 6 * DEPTH + 1, lambda k: pf[:, k:k + 1], X1)
            dve_second(dve, order, invert)

        @block.tensor
        def _(pe):
            def sums(lhs, weight):
                for i, parts in enumerate(lhs):
                    for n, part in enumerate(parts):
                        last = pe.matmul(ps[:, 7, i:i + 1], part, weight, start=(n == 0), stop=(n == len(parts) - 1))
                last.then_inc(sums_ready, 1)

            def spread(bank, first, n):
                for i in range(n):
                    last = pe.matmul(ps[:, bank + i // 4, i % 4 * P:(i % 4 + 1) * P],
                                     scales[:, first + i:first + i + 1].to_broadcast([P, P]), ident, start=True, stop=True)
                last.then_inc(spread_ready, 1)

            def norm_of_x(norm, squared):
                pe.wait_ge(squares_ready, squared)
                sums([[sq1[:, k, t * P:(t + 1) * P] for k in range(KD)] for t in range(2)], T("inv_d"))
                pe.wait_ge(scale_ready, norm + 1)
                spread(4, 0, 2)

            def panel(j, loads, frees, c, rhs, n_tok, part=(0, KD), k_all=KD, ready=None):
                s = j % SLOTS
                k0, kn = part
                pe.wait_ge(panel_loaded[s], loads)
                for n in range(2):
                    b = (c + n) % BANKS
                    if k0 == 0:
                        pe.wait_ge(drained[b], frees[n])
                    for k in range(kn):
                        if ready and n == 0:
                            pe.wait_ge(ready[0], ready[1] + k + 1)
                        last = pe.matmul(ps[:, b, 0:n_tok], W[:, s, k, n * P:(n + 1) * P], rhs(k0 + k),
                                         start=(k0 + k == 0), stop=(k0 + k == k_all - 1))
                last.then_inc(panels_done, 1)

            def loads1(l, j):
                return l * (16 * P1_ALL // SLOTS) + 16 * (j // SLOTS + 1)

            def panel1(l, j, c, rhs, turn=0, **more):
                turn_c = more.pop("turn_c", 0)
                panel(j, loads1(l, j) + 16 * (6 // SLOTS) * turn, [out_of(l, c + n - BANKS) + turn_c for n in range(2)], c,
                      lambda k: rhs[:, k, 0:SEQ], SEQ, **more)

            def problems(bank, lhs, rhs):
                for e in range(NE):
                    last = pe.matmul(ps[:, bank + e // 4, e % 4 * P:(e % 4 + 1) * P], lhs(e), rhs(e), start=True, stop=True)
                return last

            def heads(bank, *products):
                for h in range(HEADS):
                    for n, (lhs, rhs) in enumerate(products):
                        last = pe.matmul(ps[:, bank, h * P:(h + 1) * P], lhs(h), rhs(h), start=(n == 0), stop=(n == len(products) - 1))
                return last

            def ada_columns(l, jj):
                for n in range(2):
                    c = 2 * (2 * jj + n)
                    last = pe.matmul(ps[:, 3, c:c + 2], ada_rows(jj)[:, n * P:(n + 1) * P], ident[0:2, 0:2], start=True, stop=True)
                last.then_inc(ada_turned, 1)

            def ada(l, jj):
                j = P1_ADA + jj
                s = j % SLOTS
                pe.wait_ge(panel_loaded[s], loads1(l, j))
                if jj >= ADA_BANKS:
                    pe.wait_ge(ada_out, N_ADA * l + (jj - ADA_BANKS + 1))
                    ada_columns(l, jj - ADA_BANKS)
                for k in range(KD):
                    last = pe.matmul(ps[0:2, jj % ADA_BANKS, 0:PC], cnd[:, k, :], W[:, s, k, :], start=(k == 0), stop=(k == KD - 1))
                last.then_inc(panels_done, 1)

            def tile_of(v, first):
                return lambda e: v[:, first + e % HEADS, e // HEADS * P:(e // HEADS + 1) * P]

            pe.wait_ge(loaded, 32)
            pe.wait_ge(cond_ready, 1)
            with pe.Fori(0, DEPTH) as l:
                norm = l * N1_ALL
                norm_of_x(norm + N1_IN, 8 * l + 2)
                pe.wait_ge(h_ready, 16 * l + 8)
                for j in range(2):
                    pe.wait_ge(panel_loaded[P1_BA + j], loads1(l, P1_BA + j))
                    for k in range(KD // 2):
                        last = pe.matmul(ps[0:NE, 5, 0:SEQ], W[:, P1_BA + j, k, 0:NE], H1[:, KD // 2 * j + k, :],
                                         start=(j == 0 and k == 0), stop=(j == 1 and k == KD // 2 - 1))
                    last.then_inc(panels_done, 1)
                for j in range(2):
                    panel1(l, P1_QKV + j, C1_QKV + 2 * j, H1)
                pe.wait_ge(ba_out, l + 1)
                for t in range(2):
                    last = pe.matmul(ps[:, 6, NE * t:NE * (t + 1)], ba_rows[:, t * P:(t + 1) * P], ident[0:NE, 0:NE], start=True, stop=True)
                last.then_inc(ba_turned, 1)
                for j in range(2, 8):
                    panel1(l, P1_QKV + j, C1_QKV + 2 * j, H1)
                pe.wait_ge(squares_ready, 8 * l + 4)
                sums([[sq1[:, c, t * P:(t + 1) * P]] for c in range(8) for t in range(2)], T("one"))
                for j in range(2):
                    panel1(l, P1_GC + j, C1_GC + 2 * j, H1)
                pe.wait_ge(scale_ready, norm + (N1_L2 + 1))
                spread(4, 0, 8)
                spread(6, 8, 8)
                for j in range(2):
                    panel1(l, P1_HV + j, C1_HV + 2 * j, H1)
                pe.wait_ge(qk_ready, 2 * l + 2)
                pe.wait_ge(silu_ready, 12 * l + 12)
                for bank, first in ((4, HEADS), (6, 2 * HEADS)):
                    src = tile_of(qkv, first)
                    for e in range(NE):
                        last = pe.transpose(ps[:, bank + e // 4, e % 4 * P:(e % 4 + 1) * P], src(e), ident)
                    last.then_inc(turned, 1)
                for j in range(2):
                    panel1(l, P1_GB + j, C1_GB + 2 * j, H1)
                pe.wait_ge(g_ready, l + 1)
                pe.wait_ge(vtok_ready, l + 1)
                pe.matmul(ps[:, 6, 0:NE], T("upper"), glog, start=True, stop=True).then_inc(cum_ready, 1)
                pe.wait_ge(ktok_ready, l + 1)
                problems(4, lambda e: glog[:, e:e + 1].to_broadcast([P, P]), lambda e: T("upper")).then_inc(cum_ready, 1)
                for b in range(BANKS):
                    pe.wait_ge(drained[b], out_of(l, C1_GB + b))
                for jj in range(2):
                    ada(l, jj)
                pe.wait_ge(diff_ready, l + 1)
                problems(6, tile_of(qkv, HEADS), tile_of(qkv, HEADS)).then_inc(kk_ready, 1)
                ada(l, 2)
                pe.wait_ge(exps_ready, l + 1)
                problems(4, lambda e: beta[:, e:e + 1].to_broadcast([P, P]), lambda e: ident).then_inc(kk_ready, 1)
                ada(l, 3)
                pe.wait_ge(kk_used, l + 1)
                problems(6, tile_of(qkv, HEADS), tile_of(qkv, 0)).then_inc(kk_ready, 1)
                for jj in range(4, 6):
                    ada(l, jj)
                pe.wait_ge(inv_m, l * LEVELS + 1)
                for e in range(NE):
                    last = pe.transpose(ps[:, 4 + e // 4, e % 4 * P:(e % 4 + 1) * P], MT[:, e, :], ident)
                last.then_inc(inv_mm, 1)
                ada(l, 6)
                for s in range(1, LEVELS):
                    B = Bt[:, s % 2, :].rearrange("p (e c) -> p e c", e=NE)
                    pe.wait_ge(blocks_ready, l * LEVELS + (s + 1))
                    if s == 1:
                        pe.wait_ge(inv_turned, l + 1)
                    else:
                        pe.wait_ge(inv_m, l * LEVELS + s)
                    problems(4, lambda e: B[:, e, :], lambda e: M[:, e, :]).then_inc(inv_mm, 1)
                    ada(l, 5 + 2 * s)
                    pe.wait_ge(inv_y, l * (LEVELS - 1) + s)
                    if s < LEVELS - 1:
                        problems(6, lambda e: MT[:, e, :], lambda e: Y[:, e, :])
                    problems(4, lambda e: Y[:, e, :], lambda e: MT[:, e, :]).then_inc(inv_mm, 1)
                    ada(l, 6 + 2 * s)
                pe.wait_ge(inv_m, l * LEVELS + LEVELS)
                pe.wait_ge(keys_ready, l + 1)
                second = lambda v: lambda h: v[:, HEADS + h, :]
                first = lambda v: lambda h: v[:, h, :]
                heads(4, (first(MT), first(vtok))).then_inc(scan_mm, 1)
                heads(5, (first(kbg), second(MT))).then_inc(scan_mm, 1)
                ada(l, 19)
                pe.wait_ge(scan_in, 4 * l + 1)
                heads(6, (first(kdec), first(u0))).then_inc(scan_mm, 1)
                heads(7, (first(u0), first(qkT))).then_inc(scan_mm, 1)
                ada(l, 20)
                pe.wait_ge(scan_in, 4 * l + 3)
                heads(4, (second(MT), second(vtok)), (first(nw), first(S1))).then_inc(scan_mm, 1)
                ada(l, 21)
                pe.wait_ge(scan_in, 4 * l + 4)
                heads(5, (first(S1), first(qdec)), (first(vnew), second(qkT))).then_inc(scan_mm, 1)
                for jj in range(22, N_ADA):
                    ada(l, jj)
                pe.wait_ge(squares_ready, 8 * l + 6)
                sums([[sq1[:, c, t * P:(t + 1) * P]] for c in range(8) for t in range(2)], T("inv_p"))
                pe.wait_ge(ada_out, N_ADA * l + N_ADA)
                for jj in range(N_ADA - ADA_BANKS, N_ADA):
                    ada_columns(l, jj)
                pe.wait_ge(scale_ready, norm + (N1_MIX + 1))
                spread(4, 0, 8)
                spread(6, 8, 8)
                pe.wait_ge(mix_ready, l + 1)
                pe.wait_ge(mods_ready, l + 1)
                for j in range(4):
                    panel1(l, P1_OUT + j, C1_OUT + 2 * j, mix1)
                norm_of_x(norm + N1_FFN, 8 * l + 8)
                with pe.Fori(0, 3) as i:
                    pe.wait_ge(h_ready, 16 * l + 16)
                    for j in range(6):
                        panel1(l, P1_FFN + j, C1_FFN + 2 * j, H1, turn=i, turn_c=3 * i)
                for j in range(18, 22):
                    panel1(l, P1_FFN + j, C1_FFN + 2 * j, H1)
                with pe.Fori(0, 2) as i:
                    pe.wait_ge(drained[3], out_of(l, C1_FFN + 43))
                    for j in range(6):
                        panel1(l, P1_DOWN + j, C1_DOWN + j // 3 * 2, hid1, turn=i, turn_c=i, part=KPARTS[j % 3], k_all=KF)
            norm_of_x(N_FINAL, 8 * DEPTH + 2)
            pe_second(pe, sums, spread, panel)


def kernel(**inputs):
    import concourse.bacc as bacc
    from concourse.bass_utils import run_bass_kernel_spmd

    a = {n: np.asarray(v) for n, v in inputs.items()}

    def columns(v):
        return np.ascontiguousarray(v.reshape(-1, P).T)

    def layers(pack):
        return np.stack([np.concatenate(pack(l), axis=1) for l in range(DEPTH)])

    def every(v):
        return np.broadcast_to(v[None, :], (P, v.shape[0]))

    def tokens(v):
        return np.ascontiguousarray(v[0].reshape(-1, KD, P).transpose(2, 1, 0))

    vec1 = layers(lambda l: [columns(a[n][l]) for n in ("norm1_g", "dn_conv_w", "sc_conv_w", "dn_norm_g", "sc_norm_g", "norm2_g")]
                  + [every(a["dn_a_log"][l]), every(a["dn_dt_bias"][l]), columns(a["b_ada_2"][l])])
    vec2 = layers(lambda l: [columns(a[n + "_2"][l]) for n in (
        "b_in", "q_gain", "k_gain", "conv_dw_w", "conv_dw_b", "conv_ln_g", "conv_ln_b", "conv_pw_b", "pool_scale", "b_out",
        "ln1_g", "ln1_b", "ln2_g", "ln2_b", "ffn_dw_w", "ffn_dw_b")])
    cond = np.stack([columns(a["c_2"]), columns(a["c_ctx_2"])], axis=2)
    arrays = {
        "x": tokens(a["x"]), "ctx_in": tokens(a["ctx_2"]), "cond": cond, "vec1": vec1, "vec_final": columns(a["final_norm_g"]),
        "vec2": np.concatenate(list(vec2), axis=1), "tabs": tables(), "w_in": a["w_in"], "w_out": a["w_out"],
        "w_gate": a["ffn_w_gate"], "w_up": a["ffn_w_up"], "w_down": a["ffn_w_down"], "w_ada": a["w_ada_2"], "w_in2": a["w_in_2"],
        "w_pool": a["pool_w_2"], "w_pw": a["conv_pw_w_2"], "w_out2": a["w_out_2"], "w_up2": a["w_up_2"], "w_down2": a["w_down_2"],
    }
    arrays = {n: np.ascontiguousarray(v) for n, v in arrays.items()}
    nc = bacc.Bacc("TRN2", target_bir_lowering=False, num_devices=1)
    args = {n: nc.dram_tensor(n, v.shape, F32, kind="ExternalInput").ap() for n, v in arrays.items()}
    out = nc.dram_tensor("out", (P, KD, SEQ), F32, kind="ExternalOutput").ap()
    build(nc, *args.values(), out)
    r = run_bass_kernel_spmd(nc, [arrays], core_ids=[0])
    return np.ascontiguousarray(r.results[0]["out"].transpose(2, 1, 0)).reshape(1, SEQ, D)
```

```python
from contextlib import ExitStack

import concourse.bass as bass
from concourse import mybir
import numpy as np

F32 = mybir.dt.float32
F32R = mybir.dt.float32r
ALU = mybir.AluOpType
ACT = mybir.ActivationFunctionType
AX = mybir.AxisListType

P = 128
D = 1024
KD = D // P
SEQ = 256
CTX = 256
TOK = SEQ + CTX
DEPTH = 2
EPS = 1e-6
LN_EPS = 1e-5

HEADS = 4
CONV = 4
SC_CONV = 3
D_FF = 2816
KF = D_FF // P
W_IN_COLS = 3592
B_AT, SC_AT = 2048, 2056
NE = 2 * HEADS

N_HEADS, KV_HEADS = 8, 2
CW = 31
CPAD = CW // 2
POOLS = (2, 4, 8, 16)
PPAD = max(POOLS) // 2
D_IN = 7680
Q_AT, CONV_AT, GATE_AT, POOL_AT, MIX_AT = 0, 1536, 2560, 3584, 4608
ATTN_SCALE = P ** -0.5
ALPHA = (2 * DEPTH) ** 0.25
GRID_W = 64
ROPE_THETA = 10000.0
N_MOD = 6

PC = 256
SLOTS = 3
BANKS = 4
N_ADA = N_MOD * D // PC
ADA_BANKS = 3
KPARTS = ((0, 8), (8, 8), (16, 6))

P1_BA, P1_QKV, P1_Z, P1_GC, P1_HV, P1_GB, P1_ADA, P1_OUT, P1_FFN, P1_DOWN, P1_ALL = (
    0, 2, 8, 10, 12, 14, 16, 40, 44, 66, 78)
C1_QKV, C1_Z, C1_GC, C1_HV, C1_GB, C1_OUT, C1_FFN, C1_DOWN, C1_ALL = 0, 12, 16, 20, 24, 28, 36, 80, 88
P2_CONV, P2_QKV, P2_POOL, P2_G0, P2_PMIX, P2_G2, P2_PW, P2_G1, P2_OUT, P2_FFN, P2_DOWN, P2_ALL = (
    0, 8, 14, 18, 22, 26, 30, 34, 38, 42, 64, 76)
C2_CONV, C2_QKV, C2_POOL, C2_G0, C2_PMIX, C2_G2, C2_PW, C2_G1, C2_OUT, C2_FFN, C2_DOWN, C2_ALL = (
    0, 16, 28, 36, 44, 52, 60, 68, 76, 84, 128, 136)
SPLIT = [*range(P2_CONV, P2_PMIX), *range(P2_G2, P2_PW), *range(P2_G1, P2_DOWN)]
NTH = {j: q for q, j in enumerate(SPLIT)}
P2_AT, C2_AT = DEPTH * P1_ALL, DEPTH * C1_ALL
assert P1_ALL % SLOTS == 0 and C1_ALL % BANKS == 0 and C2_ALL % BANKS == 0

N1_IN, N1_L2, N1_MIX, N1_FFN, N1_ALL = 0, 1, 2, 3, 4
N_FINAL = DEPTH * N1_ALL

V1 = {}
for _name, _n in (("norm1", 8), ("dnw", 48), ("scw", 12), ("dng", 1), ("scg", 4), ("norm2", 8),
                  ("alog", 4), ("dtb", 4), ("ada", 48)):
    V1[_name] = sum(n for _, n in V1.values()), _n
V1_N = sum(n for _, n in V1.values())
V2 = {}
for _name, _n in (("bin", 60), ("qg", 1), ("kg", 1), ("cw", CW * KD), ("cb", 8), ("clg", 8),
                  ("clb", 8), ("pwb", 8), ("psc", 8), ("bout", 8), ("l1g", 8), ("l1b", 8), ("l2g", 8),
                  ("l2b", 8), ("fw", 3 * KF), ("fb", KF)):
    V2[_name] = sum(n for _, n in V2.values()), _n
V2_N = sum(n for _, n in V2.values())
LEVELS = 7
TAB = {}
for _name, _n in (("ident", P), ("upper", P), ("cap", P), ("level", LEVELS * P), ("perm", P), ("cos", SEQ),
                  ("sin", SEQ), ("one", 1), ("inv_d", 1), ("inv_p", 1), ("eps", 1),
                  ("ln_eps", 1)):
    TAB[_name] = sum(n for _, n in TAB.values()), _n
TAB_N = sum(n for _, n in TAB.values())


def tables():
    m, c = np.meshgrid(np.arange(P), np.arange(P), indexing="ij")
    t = np.arange(SEQ)
    out = {"ident": (m == c), "upper": (m <= c), "cap": np.where(m <= c, 0.0, -3e38)}
    out["level"] = np.concatenate(
        [(m // (2 << s) == c // (2 << s)) & (m % (2 << s) < (1 << s)) & (c % (2 << s) >= (1 << s))
         for s in range(LEVELS)], axis=1)
    half = (c // 32) % 2
    out["perm"] = np.where((half == 0) & (m == c + 32), -1.0, 0.0) + np.where((half == 1) & (m == c - 32), 1.0, 0.0)
    pairs = P // 4
    inv = np.float32(ROPE_THETA) ** (-np.arange(pairs, dtype=np.float32) / np.float32(pairs))
    row, col = (t // GRID_W).astype(np.float32), (t % GRID_W).astype(np.float32)
    ang = np.stack([np.outer(inv, row), np.outer(inv, col)]).astype(np.float32)
    ang = np.repeat(ang[:, None], 2, axis=1).reshape(P, SEQ)
    out["cos"], out["sin"] = np.cos(ang), np.sin(ang)
    for name, v in (("one", 1.0), ("inv_d", 1.0 / D), ("inv_p", 1.0 / P), ("eps", EPS), ("ln_eps", LN_EPS)):
        out[name] = np.full((P, 1), v)
    return np.concatenate([out[n].astype(np.float32) for n in TAB], axis=1)


def window_counts():
    t = np.arange(SEQ)
    cnt = np.stack([np.clip(t - w // 2 + w, 0, SEQ) - np.clip(t - w // 2, 0, SEQ) for w in POOLS])
    return np.broadcast_to((1.0 / cnt).astype(np.float32).reshape(1, -1), (P, len(POOLS) * SEQ))


class Order:

    def __init__(self, eng, sem):
        self.eng, self.sem, self.base, self.n, self.outer = eng, sem, 0, 0, []

    def __call__(self, ins):
        self.n += 1
        ins.then_inc(self.sem, 1)
        return self.n

    def wait(self, step=None):
        self.eng.wait_ge(self.sem, self.base + (step or self.n))

    def wait_but(self, n):
        self.wait(self.n - n)

    def enter(self, i, steps, first=0):
        self.outer.append((self.base, self.n, steps))
        self.base = i * steps + (self.base - first * steps)

    def leave(self, turns):
        base, n, steps = self.outer.pop()
        assert self.n - n == steps, ("steps of a turn", self.n - n, steps)
        self.base, self.n = base, n + steps * turns


def flat(v):
    return v.rearrange("p a b -> p (a b)")


def build(nc, x, ctx_in, cond, vec1, vec_final, vec2, tabs, counts, w_in, w_out, w_gate, w_up, w_down,
          w_ada, w_in2, w_pool, w_pw, w_out2, w_up2, w_down2, out):
    with ExitStack() as ctx:
        def sb(name, cols, kind=F32):
            return ctx.enter_context(nc.sbuf_tensor(name, [P, cols], kind))

        def sem(name):
            return ctx.enter_context(nc.semaphore(name))

        W = sb("W", SLOTS * KD * PC)[:, :].rearrange("p (s k n) -> p s k n", s=SLOTS, k=KD)
        X = sb("X", KD * TOK)[:, :].rearrange("p (k t) -> p k t", k=KD)
        Hn = sb("Hn", KD * TOK)[:, :].rearrange("p (k t) -> p k t", k=KD)
        Hhi, Hlo = (sb(n, KD * TOK, F32R)[:, :].rearrange("p (k t) -> p k t", k=KD) for n in ("Hhi", "Hlo"))
        Whi, Wlo = (sb(n, KD * PC, F32R)[:, :].rearrange("p (n k m) -> p n k m", n=2, k=KD) for n in ("Whi", "Wlo"))
        tab = sb("tab", TAB_N)
        p1 = sb("p1", V1_N)
        pf = sb("pf", KD)
        p2 = sb("p2", DEPTH * V2_N)
        cnd = sb("cnd", KD * 2)[:, :].rearrange("p (k c) -> p k c", c=2)
        mods = sb("mods", DEPTH * N_MOD * KD * 2)
        small = sb("small", 192)
        roots, scales, rates = small[:, 0:40], small[:, 40:80], small[:, 80:84]
        ARENA = 22752
        arena = sb("arena", ARENA)
        ps = ctx.enter_context(nc.psum_tensor("ps", [P, 8, 512], F32))

        at = [0]

        def take(*dims):
            n = int(np.prod(dims))
            v = arena[:, at[0]:at[0] + n]
            at[0] += n
            assert at[0] <= ARENA, at[0]
            if len(dims) == 2:
                v = v.rearrange("p (a b) -> p a b", b=dims[1])
            if len(dims) == 3:
                v = v.rearrange("p (a b c) -> p a b c", b=dims[1], c=dims[2])
            return v

        def T(name, i=0, n=None):
            a, m = TAB[name]
            return tab[:, a + i:a + i + (n or m)]

        def v1(name, i=0, n=1):
            return p1[:, V1[name][0] + i:V1[name][0] + i + n]

        def v2(L, name, i=0, n=1):
            return p2[:, bass.ds(L * V2_N + V2[name][0] + i, n)]

        ident = T("ident")

        def ada_rows(jj):
            return xpad[0:2, jj % 12, CONV - 1:]

        X1, H1 = X[:, :, 0:SEQ], Hn[:, :, 0:SEQ]
        mix1, sq1 = Hn[:, :, SEQ:TOK], X[:, :, SEQ:TOK]
        ktok = take(NE, P)
        vtok = take(NE, P)
        DT = take(NE, P)
        AT = take(NE, P)
        Bt = take(2, NE * P)
        hid1 = arena[:, 0:KF * SEQ].rearrange("p (k t) -> p k t", k=KF)
        assert KF * SEQ <= at[0]
        xpad = take(12, SEQ + CONV - 1)
        qkv = take(12, SEQ)
        zs = take(HEADS, SEQ)
        spad = take(HEADS, SEQ + SC_CONV - 1)
        gc = take(HEADS, SEQ)
        gb = take(HEADS, SEQ)
        ysc = take(HEADS, SEQ)
        qkT = take(NE, P)
        M = take(NE, P)
        MT = take(NE, P)
        Y = take(NE, P)
        qdec = take(HEADS, P)

        def four(v):
            return flat(v).rearrange("p (h c) -> p h c", h=HEADS)

        kbg, kdec = four(gc[:, 0:2, :]), four(gc[:, 2:4, :])
        S1, nw = four(qkv[:, 4:6, :]), four(qkv[:, 6:8, :])
        u0, vnew = four(qkv[:, 8:10, :]), four(qkv[:, 10:12, :])
        odn = flat(Y).rearrange("p (h t) -> p h t", h=HEADS)
        gs1 = take(2, SEQ)
        ba_rows = gs1[0:NE, 0, :]
        cols = take(9, NE)
        beta, gin, gabs, gexp, gsp, gmax, glog, gcol, egc = (cols[:, i, :] for i in range(9))
        bge = take(1, NE)[:, 0, :]

        at[0] = 0
        qk = take(10, TOK)
        vt2 = take(4, KV_HEADS * P)
        prob = take(2, TOK)
        probT = take(2, TOK)
        vT = prob
        ksq = flat(probT).rearrange("p (a b) -> p a b", b=TOK)
        rope = flat(probT).rearrange("p (a b) -> p a b", b=SEQ)
        GATES = 3
        sg = take(GATES, TOK)
        ptmp = flat(sg)[:, 0:4 * (SEQ + 2 * PPAD)].rearrange("p (a b c) -> p a b c", a=2, b=2)
        lo = at[0]
        cbuf = take(KD, 2, SEQ + 2 * CPAD)
        pbuf = take(KD, 2, SEQ + 2 * PPAD)
        pooled = take(KD, TOK)
        hid2 = arena[:, lo:lo + KF * TOK].rearrange("p (k t) -> p k t", k=KF)
        n_abuf = 2 * 2 * (SEQ + 2)
        assert lo + KF * TOK <= at[0] - n_abuf
        abuf = arena[:, at[0] - n_abuf:at[0]].rearrange("p (a b c) -> p a b c", a=2, b=2)
        Hraw = (pooled, Hn)
        co = (Hn, pbuf[:, :, 1, 0:SEQ])
        stat = small[:, 84:108].rearrange("p (a b) -> p a b", b=4)
        bmod = [small[:, a:a + 2 * KD].rearrange("p (k c) -> p k c", c=2) for a in (108, 108 + 2 * KD)]

        loaded = sem("x_and_tables_loaded")
        cond_loaded, vec2_loaded = sem("cond_loaded"), sem("vec2_loaded")
        vec1_loaded, ctx_loaded = sem("vec1_loaded"), sem("ctx_loaded")
        panel_loaded = [sem(f"panel_loaded{s}") for s in range(SLOTS)]
        panels_done = sem("panels_done")
        drained = [sem(f"drained{b}") for b in range(BANKS)]
        act_order, dve_order, pool_order = sem("act_order"), sem("dve_order"), sem("pool_order")
        square_sum_ready = sem("square_sum_ready")
        squares_ready, sums_ready, root_ready, scale_ready, spread_ready = (
            sem(n) for n in ("squares_ready", "sums_ready", "root_ready", "scale_ready", "spread_ready"))
        h_ready, cond_ready, mods_ready = sem("h_ready"), sem("cond_ready"), sem("mods_ready")
        ba_out, ba_turned = sem("ba_out"), sem("ba_turned")
        ada_out, ada_turned = sem("ada_out"), sem("ada_turned")
        beta_ready, gin_ready, log_ready, g_ready = sem("beta_ready"), sem("gin_ready"), sem("log_ready"), sem("g_ready")
        conv1_ready, silu_ready = sem("conv1_ready"), sem("silu_ready")
        qk_ready, turned, ktok_ready, vtok_ready = sem("qk_ready"), sem("turned"), sem("ktok_ready"), sem("vtok_ready")
        cum_ready, diff_ready, decay_ready, exps_ready, kk_ready, kk_used, at_ready = (
            sem(n) for n in ("cum_ready", "diff_ready", "decay_ready", "exps_ready", "kk_ready", "kk_used", "at_ready"))
        blocks_ready, inv_mm, inv_turned, inv_y, inv_m = (
            sem(n) for n in ("blocks_ready", "inv_mm", "inv_turned", "inv_y", "inv_m"))
        keys_ready, scan_mm, scan_in = sem("keys_ready"), sem("scan_mm"), sem("scan_in")
        hi_done, split_done, halves_done = sem("hi_done"), sem("split_done"), sem("halves_done")
        hhi_ready, hlo_ready, counts_loaded = sem("hhi_ready"), sem("hlo_ready"), sem("counts_loaded")
        y_ready, mix_ready, stored, layer_opened = sem("y_ready"), sem("mix_ready"), sem("stored"), sem("layer_opened")

        block = ctx.enter_context(nc.Block())

        SQ1_ALL = 20


        def done(l, j):
            return l * P1_ALL + (SLOTS + j + 1)

        def out_of(l, c):
            return l * (C1_ALL // BANKS) + (c // BANKS + 2)

        def done2(L, j):
            return P2_AT + L * P2_ALL + SLOTS + j + 1

        def out_of2(L, c):
            return (C2_AT + L * C2_ALL + c) // BANKS + 2

        def rows(w, k0=0, n=KD):
            return w.rearrange("(k p) n -> p k n", p=P)[:, k0:k0 + n, :]

        h2_ready, x2_ready, pads_ready = sem("h2_ready"), sem("x2_ready"), sem("pads_ready")
        rotated, perm_ready, rope_done = sem("rotated"), sem("perm_ready"), sem("rope_done")
        score_mm, max_ready, exp_ready, prob_ready = (sem(n) for n in ("score_mm", "max_ready", "exp_ready", "prob_ready"))
        turn_mm, probT_ready, o_mm, attn_ready = (sem(n) for n in ("turn_mm", "probT_ready", "o_mm", "attn_ready"))
        v_turned, v_ready, pooled_ready, gated = sem("v_turned"), sem("v_ready"), sem("pooled_ready"), sem("gated")
        total_ready, centred, lnorm_ready, lsilu_ready = sem("total_ready"), sem("centred"), sem("lnorm_ready"), sem("lsilu_ready")
        pairs_ready = sem("pairs_ready")
        aconv_ready, asilu_ready = sem("aconv_ready"), sem("asilu_ready")

        def width(L):
            return TOK if L == 0 else SEQ

        def streams(v, L):
            return v.rearrange("p (s t) -> p s t", t=SEQ)

        def mod(L, m, k, s):
            a = ((L * N_MOD + m) * KD + k) * 2 + s
            return mods[:, a:a + 1]

        def qk_tiles(L):
            return [(c, t) for c in range(10) for t in range(width(L) // P if c < N_HEADS else TOK // P)]

        def items(L):
            return [(h, t, 0 if t < 2 else SEQ, TOK if t < 2 else CTX) for h in range(N_HEADS) for t in range(width(L) // P)]

        def items_before(L):
            return sum(len(items(n)) for n in range(L))

        O_BANKS = (3, 7)
        T_BANKS = (6, 2)
        SUM2 = DEPTH * N1_ALL + 1
        S_QK, S_CONV, S_LN1, S_LN2, S_ALL = 0, 1, 3, 5, 7
        R_QK, R_CONV, R_LN1, R_LN2, R_ALL = 0, 1, 2, 3, 4
        SQ2, SQ_ALL = KD + SQ1_ALL * DEPTH, 14
        SP2, SP_ALL = 6 * DEPTH + 1, 16

        PAIRS = KD // 2
        total = pooled[:, 5, :]

        def load_second(sp, load):
            for L in range(DEPTH):
                wi = rows(w_in2[L])
                at_ = P2_AT + L * P2_ALL

                def put(j, src):
                    load(at_ + j, at_ + j, src, split=NTH.get(j - SLOTS) if L == 0 else None)

                def four(j, first):
                    for n in range(4):
                        put(j + n, wi[:, :, first + n * PC:first + (n + 1) * PC])

                for j in range(4):
                    for n, first in enumerate((CONV_AT, GATE_AT)):
                        put(P2_CONV + 2 * j + n, wi[:, :, first + j * PC:first + (j + 1) * PC])
                for j in range(6):
                    put(P2_QKV + j, wi[:, :, Q_AT + j * PC:Q_AT + (j + 1) * PC])
                four(P2_POOL, POOL_AT)
                four(P2_G0, MIX_AT)
                for j in range(4):
                    put(P2_PMIX + j, rows(w_pool[L, j], 0, 2))
                four(P2_G2, MIX_AT + 2 * D)
                for j in range(4):
                    put(P2_PW + j, rows(w_pw[L])[:, :, j * PC:(j + 1) * PC])
                four(P2_G1, MIX_AT + D)
                for j in range(4):
                    put(P2_OUT + j, rows(w_out2[L])[:, :, j * PC:(j + 1) * PC])
                wu, wd = rows(w_up2[L]), w_down2[L]
                for j in range(4):
                    first = j % 2 * D_FF + j // 2 * PC
                    put(P2_FFN + j, wu[:, :, first:first + PC])
                with sp.Fori(0, 3) as i:
                    for j in range(4, 10):
                        load(6 * i + (at_ + P2_FFN + j), at_ + P2_FFN + j,
                             wu[:, :, bass.ds(3 * i * PC + (j % 2 * D_FF + j // 2 * PC), PC)],
                             split=6 * i + NTH[P2_FFN + j - SLOTS] if L == 0 else None)
                with sp.Fori(0, 2) as i:
                    for j in range(6):
                        load(6 * i + (at_ + P2_DOWN + j), at_ + P2_DOWN + j,
                             rows(wd, *KPARTS[j % 3])[:, :, bass.ds((2 * i + j // 3) * PC, PC)])
            sp.wait_ge(x2_ready, 1)

        def pool_second(pool):
            order = Order(pool, pool_order)
            pool.wait_ge(sums_ready, N_FINAL + 1)
            pool.dma_start(X[:, :, SEQ:TOK], ctx_in).then_inc(ctx_loaded, 16)
            pool.dma_start(T("cap", 0, len(POOLS) * SEQ), counts).then_inc(counts_loaded, 16)

            def lo(q, n, j):
                pool.wait_ge(hi_done, 2 * q + (n + 1))
                pool.tensor_tensor(Wlo[:, n], W[:, (P2_AT + j) % SLOTS, :, n * P:(n + 1) * P], Whi[:, n], ALU.subtract).then_inc(split_done, 1)

            def lows(first, end):
                for q in range(first, end):
                    for n in range(2):
                        lo(q, n, SPLIT[q])

            for L in range(DEPTH):
                S = width(L) // SEQ
                pool.wait_ge(drained[3], out_of2(L, -1))
                for buf, pad in ((cbuf, CPAD), (pbuf, PPAD)):
                    for a in (0, pad + SEQ):
                        pool.memset(buf[:, :, 0:S, a:a + pad], 0.0).then_inc(pads_ready, 1)
                if L == 0:
                    lows(0, NTH[P2_G0] + 1)
                pool.wait_ge(pads_ready, 4 * L + 4)
                pool.wait_ge(counts_loaded, 16)
                pool.wait_ge(sums_ready, SUM2 + S_ALL * L + S_QK + 1)
                for c in range(KD):
                    g = c // 2
                    pool.wait_ge(drained[c % BANKS], out_of2(L, C2_POOL + c))
                    w, size = pbuf[:, c, 0:S, :], 1
                    for n in range(g + 1):
                        keep = SEQ + 2 * PPAD - 2 * size + 1
                        dst = ptmp[:, n % 2, 0:S, 0:keep]
                        order(pool.tensor_tensor(dst, w[:, :, 0:keep], w[:, :, size:size + keep], ALU.add))
                        order.wait()
                        w, size = dst, 2 * size
                    a = PPAD - size // 2
                    dst = streams(pooled[:, c, 0:S * SEQ], L)
                    order(pool.tensor_tensor(dst, w[:, :, a:a + SEQ], T("cap", g * SEQ, SEQ).unsqueeze(1).to_broadcast([P, S, SEQ]), ALU.mult))
                    order.wait()
                    pool.tensor_tensor(dst, dst, pbuf[:, c, 0:S, PPAD:PPAD + SEQ], ALU.subtract).then_inc(pooled_ready, 1)
                if L == 0:
                    lows(NTH[P2_G0] + 1, NTH[P2_FFN])
                    with pool.Fori(0, 3) as i:
                        for j in range(6):
                            for n in range(2):
                                lo(6 * i + NTH[P2_FFN + j], n, P2_FFN + j)
                    lows(NTH[P2_FFN + 18], len(SPLIT))

        def act_second(act, order, squares, root):
            def chunk(L, j, c, n):
                act.wait_ge(panels_done, done2(L, j))
                return ps[:, c % BANKS, 0:n]

            def hi(j, n, turn=0):
                slot, q = (P2_AT + j) % SLOTS, NTH[j]
                if n == 0:
                    act.wait_ge(panel_loaded[slot], 16 * (6 // SLOTS) * turn + 16 * ((P2_AT + j) // SLOTS + 1))
                if q and n == 0:
                    act.wait_ge(halves_done, 6 * turn + q)
                elif q:
                    act.wait_ge(panels_done, 6 * turn + done2(0, SPLIT[q - 1]))
                act.activation(Whi[:, n], W[:, slot, :, n * P:(n + 1) * P], ACT.Copy).then_inc(hi_done, 1)

            def ahead(L, j, turn=0):
                if L == 0:
                    for n in range(2):
                        hi(j, n, turn)

            def round_input(src, ready, count):
                for k in range(KD):
                    act.wait_ge(ready, count + k + 1)
                    act.activation(Hhi[:, k, :], src[:, k, :], ACT.Copy).then_inc(hhi_ready, 1)

            ahead(0, P2_CONV)
            for L in range(DEPTH):
                n_tok = width(L)
                S = n_tok // SEQ
                if L == 0:
                    round_input(Hraw[0], h2_ready, 0)
                for j in range(4):
                    for m in range(2):
                        ahead(L, P2_CONV + 2 * j + m + 1)
                    for c in range(2):
                        src = chunk(L, P2_CONV + 2 * j + 1, 2 + c, n_tok)
                        if j:
                            act.wait_ge(drained[c], out_of2(L, C2_CONV + 4 * (j - 1) + c))
                        act.activation(sg[:, c, 0:n_tok], src, ACT.Sigmoid, bias=v2(L, "bin", 20 + 2 * j + c)).then_inc(drained[2 + c], 1)
                for c in range(12):
                    n = n_tok if c < N_HEADS else TOK
                    if c % 2 == 0:
                        ahead(L, P2_QKV + c // 2 + 1)
                    dst = qk[:, c, 0:n] if c < 10 else vT[:, c - 10, 0:n]
                    act.activation(dst, chunk(L, P2_QKV + c // 2, c, n), ACT.Identity, bias=v2(L, "bin", c)).then_inc(drained[c % BANKS], 1)
                act.wait_ge(drained[1], out_of2(L, C2_QKV + 9))
                squares(pooled[:, :, 0:n_tok], qk[:, 0:N_HEADS, 0:n_tok])
                squares(ksq, qk[:, N_HEADS:10, :])
                act.wait_ge(pads_ready, 4 * L + 4)
                for c in range(KD):
                    if c % 2 == 0:
                        ahead(L, P2_POOL + c // 2 + 1)
                    src = streams(chunk(L, P2_POOL + c // 2, c, n_tok), L)
                    act.activation(pbuf[:, c, 0:S, PPAD:PPAD + SEQ], src, ACT.Identity, bias=v2(L, "bin", 28 + c)).then_inc(drained[c % BANKS], 1)
                act.wait_ge(v_turned, L + 1)
                act.activation(flat(vt2), flat(ps[:, 4:6, :]), ACT.Copy).then_inc(v_ready, 1)
                root([SUM2 + S_ALL * L + S_QK], len(qk_tiles(L)))
                todo, a0 = items(L), items_before(L)

                def exp(i):
                    act.wait_ge(max_ready, a0 + i + 1)
                    if i >= 2:
                        act.wait_ge(turn_mm, a0 + i - 1)
                    n = todo[i][3]
                    act.activation(prob[:, i % 2, 0:n], ps[:, 4 + i % 2, 0:n], ACT.Exp, bias=stat[:, 1, i % 4:i % 4 + 1], scale=ATTN_SCALE,
                                   accum_out=stat[:, 2, i % 4:i % 4 + 1]).then_inc(exp_ready, 1)

                def output(i):
                    h, t, _, _ = todo[i]
                    act.wait_ge(o_mm, a0 + i + 1)
                    act.activation(qk[:, h, t * P:(t + 1) * P], ps[:, O_BANKS[i % 2], 0:P], ACT.Copy).then_inc(attn_ready, 1)

                exp(0)
                for i in range(len(todo)):
                    if i + 1 < len(todo):
                        exp(i + 1)
                    act.wait_ge(turn_mm, a0 + i + 1)
                    if i >= 2:
                        act.wait_ge(o_mm, a0 + i - 1)
                    n = todo[i][3]
                    act.activation(probT[:, i % 2, 0:n], ps[:, T_BANKS[i % 2], 0:n], ACT.Copy).then_inc(probT_ready, 1)
                    if i:
                        output(i - 1)
                output(len(todo) - 1)

                def gates(j, c0, first, nth, start=0, end=KD):
                    for c in range(start, end):
                        if c % 2 == 0 and c < KD - 2:
                            ahead(L, j + c // 2 + 1)
                        src = chunk(L, j + c // 2, c0 + c, n_tok)
                        g = 24 * L + KD * nth + c
                        if g >= GATES:
                            act.wait_ge(gated, g - GATES + 1)
                        act.activation(sg[:, g % GATES, 0:n_tok], src, ACT.Sigmoid, bias=v2(L, "bin", first + c)).then_inc(drained[c % BANKS], 1)

                act.wait_ge(pooled_ready, KD * (L + 1))
                gates(P2_G0, C2_G0, 36, 0)
                for c in range(KD):
                    src = streams(chunk(L, P2_PMIX + c // 2, c, n_tok), L)
                    act.activation(pbuf[:, c, 0:S, PPAD:PPAD + SEQ], src, ACT.Copy, scale=v2(L, "psc", c)).then_inc(drained[c % BANKS], 1)
                    if c == 5:
                        ahead(L, P2_G2)
                def pair_squares(nth, src):
                    for k in range(PAIRS):
                        act.wait_ge(centred, (3 * L + nth) * PAIRS + k + 1)
                        squares(pooled[:, 2 * k:2 * k + 2, 0:n_tok], src[:, 2 * k:2 * k + 2, 0:n_tok])

                def variance_root(s_at):
                    root([SUM2 + S_ALL * L + s_at + 1], n_tok // P, "ln_eps")

                gates(P2_G2, C2_G2, 52, 1, 0, 2)
                pair_squares(0, co[L])
                gates(P2_G2, C2_G2, 52, 1, 2, 4)
                variance_root(S_CONV)
                gates(P2_G2, C2_G2, 52, 1, 4, 6)
                for c in range(KD):
                    act.wait_ge(lnorm_ready, KD * L + c + 1)
                    act.activation(co[L][:, c, 0:n_tok], co[L][:, c, 0:n_tok], ACT.Silu, scale=v2(L, "clg", c), bias=v2(L, "clb", c)).then_inc(lsilu_ready, 1)
                gates(P2_G2, C2_G2, 52, 1, 6, 8)
                for c in range(KD):
                    src = streams(chunk(L, P2_PW + c // 2, c, n_tok), L)
                    act.activation(cbuf[:, c, 0:S, CPAD:CPAD + SEQ], src, ACT.Identity, bias=v2(L, "pwb", c)).then_inc(drained[c % BANKS], 1)
                    if c == 5:
                        ahead(L, P2_G1)
                gates(P2_G1, C2_G1, 44, 2)
                if L == 0:
                    ahead(L, P2_OUT)
                    round_input(qk, gated, 16)
                for j in range(4):
                    ahead(L, P2_OUT + j + 1)
                pair_squares(1, X)
                variance_root(S_LN1)
                if L == 0:
                    round_input(Hraw[0], h2_ready, KD)

                def ffn_turn(j, i, turn, last=False):
                    ahead(L, j + 1, turn)
                    for c in range(2):
                        act.wait_ge(panels_done, 2 * i + done2(L, P2_FFN))
                        act.wait_ge(aconv_ready, 2 * i + (2 * (KF // 2) * L + 2))
                        act.activation(abuf[:, c, 0:S, 1:1 + SEQ], streams(ps[:, c, 0:n_tok], L), ACT.Copy).then_inc(drained[c], 1)
                    if L == 0 and not last:
                        hi(j + 2, 0, turn)
                    for c in range(2):
                        act.wait_ge(aconv_ready, 2 * i + (2 * (KF // 2) * L + 2 + c + 1))
                        act.activation(sg[:, c, 0:n_tok], sg[:, c, 0:n_tok], ACT.Silu).then_inc(asilu_ready, 1)
                    if L == 0 and not last:
                        hi(j + 2, 1, turn)

                with act.Fori(0, 3) as i:
                    for m in range(3):
                        ffn_turn(P2_FFN + 2 * m, 3 * i + m, i)
                for m in range(9, KF // 2):
                    ffn_turn(P2_FFN + 2 * m, m, 0, last=(m == KF // 2 - 1))
                pair_squares(2, X)
                variance_root(S_LN2)

        def prepare_modulation(dve, order):
            dve.wait_ge(mods_ready, DEPTH)
            for L in range(DEPTH):
                for m in (1, 4):
                    a = (L * N_MOD + m) * KD * 2
                    order(dve.tensor_scalar(mods[:, a:a + 2 * KD], mods[:, a:a + 2 * KD], 1.0, None, ALU.add))
                a = (L * N_MOD + 2) * KD * 2
                order(dve.tensor_tensor(bmod[L], mods[:, a:a + 2 * KD].rearrange("p (k c) -> p k c", c=2),
                                        v2(L, "bout", 0, KD).unsqueeze(2).to_broadcast([P, KD, 2]), ALU.mult))
            order.wait()

        def dve_second(dve, order, invert):
            def chunk(L, j, c, n):
                dve.wait_ge(panels_done, done2(L, j))
                return ps[:, c % BANKS, 0:n]

            dve.sem_inc(aconv_ready, 2)
            for L in range(DEPTH):
                n_tok = width(L)
                S = n_tok // SEQ
                tiles = n_tok // P
                lo_, hi_ = (lambda s: s * SEQ), (lambda s: (s + 1) * SEQ)
                if L == 0:
                    dve.wait_ge(h_ready, 16 * DEPTH + 8)
                    dve.wait_ge(ctx_loaded, 16)
                def rest(m, k, src):
                    dve.wait_ge(hhi_ready, KD * m + k + 1)
                    dve.tensor_tensor(Hlo[:, k, :], src[:, k, :], Hhi[:, k, :], ALU.subtract).then_inc(hlo_ready, 1)

                def modulate(n_streams, m, nth_input, step=None):
                    lag = 2 if L == 0 else 0
                    for k in range(KD + lag):
                        if k < KD:
                            if step:
                                order.wait(step(k))
                            for s in range(n_streams):
                                ins = dve.tensor_scalar(Hraw[L][:, k, lo_(s):hi_(s)], X[:, k, lo_(s):hi_(s)], mod(L, m + 1, k, s), mod(L, m, k, s),
                                                        ALU.mult, ALU.add)
                            ins.then_inc(h2_ready, 1)
                        if lag and k >= lag:
                            rest(nth_input, k - lag, Hraw[0])

                modulate(2, 0, 0, step if L else None)
                dve.wait_ge(h2_ready, 2 * KD * L + KD)
                for k in range(KD):
                    for s in range(S):
                        order(dve.tensor_scalar(X[:, k, lo_(s):hi_(s)], X[:, k, lo_(s):hi_(s)], ALPHA, bmod[L][:, k, s:s + 1], ALU.mult, ALU.add))
                for j in range(4):
                    for c in range(2):
                        dve.wait_ge(drained[2 + c], out_of2(L, C2_CONV + 4 * j + 2 + c))
                        k = 2 * j + c
                        dve.scalar_tensor_tensor(out=cbuf[:, k, 0:S, CPAD:CPAD + SEQ], in0=streams(ps[:, c, 0:n_tok], L), scalar=v2(L, "bin", 12 + k),
                                                 in1=streams(sg[:, c, 0:n_tok], L), op0=ALU.add, op1=ALU.mult).then_inc(drained[c], 1)
                dve.wait_ge(drained[1], out_of2(L, C2_CONV + 13))
                dve.wait_ge(pads_ready, 4 * L + 4)

                def tap(i, j):
                    for c in range(2):
                        src = cbuf[:, bass.ds(2 * i + c, 1), 0:S, j:j + SEQ].rearrange("p a s t -> p (a s) t")
                        acc = streams(flat(co[L][:, bass.ds(2 * i + c, 1), 0:n_tok]), L)
                        w = v2(L, "cw", 2 * i + (j * KD + c))
                        if j == 0:
                            order(dve.tensor_scalar(acc, src, w, v2(L, "cb", 2 * i + c), ALU.mult, ALU.add))
                        else:
                            order.wait_but(1)
                            order(dve.scalar_tensor_tensor(out=acc, in0=src, scalar=w, in1=acc, op0=ALU.mult, op1=ALU.add))

                with dve.Fori(0, 2) as i:
                    order.enter(i, 2 * CW)
                    for j in range(CW):
                        tap(i, j)
                    order.leave(2)
                early = CW - 4
                for j in range(early):
                    tap(2, j)
                invert([SUM2 + R_ALL * L + R_QK], len(qk_tiles(L)))
                for c in range(10):
                    n = n_tok if c < N_HEADS else TOK
                    b = 4 + c % 3
                    dve.wait_ge(spread_ready, SP2 + SP_ALL * L + c + 1)
                    dve.scalar_tensor_tensor(out=qk[:, c, 0:n], in0=qk[:, c, 0:n], scalar=v2(L, "qg" if c < N_HEADS else "kg"),
                                             in1=ps[:, b, 0:n], op0=ALU.mult, op1=ALU.mult).then_inc(rotated, 1)
                    dve.wait_ge(rotated, 10 * L + c + 1)
                    order(dve.tensor_tensor(rope[:, 0, :], qk[:, c, 0:SEQ], T("cos"), ALU.mult))
                    dve.wait_ge(perm_ready, 10 * L + c + 1)
                    order(dve.tensor_tensor(rope[:, 1, :], ps[:, b, 0:SEQ], T("sin"), ALU.mult))
                    order.wait()
                    dve.tensor_tensor(qk[:, c, 0:SEQ], rope[:, 0, :], rope[:, 1, :], ALU.add).then_inc(rope_done, 1)
                    dve.wait_ge(rope_done, 10 * L + c + 1)
                todo, a0 = items(L), items_before(L)

                def maximum(i):
                    s, n = i % 4, todo[i][3]
                    dve.wait_ge(score_mm, a0 + i + 1)
                    order(dve.tensor_reduce(stat[:, 0, s:s + 1], ps[:, 4 + i % 2, 0:n], AX.X, ALU.max))
                    order.wait()
                    dve.tensor_scalar(stat[:, 1, s:s + 1], stat[:, 0, s:s + 1], -ATTN_SCALE, None, ALU.mult).then_inc(max_ready, 1)

                maximum(0)
                for i in range(len(todo)):
                    if i + 1 < len(todo):
                        maximum(i + 1)
                    s, n = i % 4, todo[i][3]
                    dve.wait_ge(exp_ready, a0 + i + 1)
                    order(dve.reciprocal(stat[:, 3, s:s + 1], stat[:, 2, s:s + 1]))
                    order.wait()
                    dve.tensor_scalar(prob[:, i % 2, 0:n], prob[:, i % 2, 0:n], stat[:, 3, s:s + 1], None, ALU.mult).then_inc(prob_ready, 1)
                dve.wait_ge(attn_ready, a0 + len(todo))
                for c in range(KD):
                    g = 24 * L + c
                    dve.wait_ge(drained[c % BANKS], out_of2(L, C2_G0 + c))
                    dve.tensor_tensor(qk[:, c, 0:n_tok], qk[:, c, 0:n_tok], sg[:, g % GATES, 0:n_tok], ALU.mult).then_inc(gated, 1)
                    if c == 0:
                        for j in range(early, CW):
                            tap(2, j)
                    for j in range(4 * c, min(4 * c + 4, CW)):
                        tap(3, j)

                def add_branch(nth, c0, branch, first=0, end=KD):
                    for c in range(first, end):
                        g = 24 * L + KD * nth + c
                        dve.wait_ge(drained[c % BANKS], out_of2(L, c0 + c))
                        v = streams(sg[:, g % GATES, 0:n_tok], L)
                        order(dve.tensor_tensor(v, v, branch(c), ALU.mult))
                        order.wait()
                        if g >= KD:
                            dve.wait_ge(gated, g - KD + 1)
                        dve.tensor_tensor(qk[:, c, 0:n_tok], qk[:, c, 0:n_tok], sg[:, g % GATES, 0:n_tok], ALU.add).then_inc(gated, 1)

                order.wait()
                dve.wait_ge(panels_done, done2(L, P2_PMIX + 3))
                for k in range(1, KD):
                    ins = dve.tensor_tensor(total[:, 0:n_tok], total[:, 0:n_tok] if k > 1 else co[L][:, 0, 0:n_tok], co[L][:, k, 0:n_tok], ALU.add)
                    if k < KD - 1:
                        order(ins)
                        order.wait()
                    else:
                        ins.then_inc(total_ready, 1)

                def mean(s_at):
                    dve.wait_ge(sums_ready, SUM2 + S_ALL * L + s_at + 1)
                    dve.tensor_copy(scales[:, 0:tiles], ps[:, 7, 0:tiles]).then_inc(scale_ready, 1)

                def centre(nth, sp_at, src):
                    dve.wait_ge(spread_ready, SP2 + SP_ALL * L + sp_at + 1)
                    for k in range(PAIRS + 1):
                        if k < PAIRS:
                            for c in (2 * k, 2 * k + 1):
                                ins = dve.tensor_tensor(src[:, c, 0:n_tok], src[:, c, 0:n_tok], ps[:, 4, 0:n_tok], ALU.subtract)
                            ins.then_inc(centred, 1)
                        if k:
                            v = pooled[:, 2 * k - 2:2 * k, 0:n_tok]
                            dve.wait_ge(squares_ready, SQ2 + SQ_ALL * L + 2 + PAIRS * nth + k)
                            dve.tensor_tensor(v[:, 0, :], v[:, 0, :], v[:, 1, :], ALU.add).then_inc(pairs_ready, 1)
                    dve.wait_ge(centred, (3 * L + nth + 1) * PAIRS)

                def deviation(nth):
                    invert([SUM2 + R_ALL * L + R_CONV + nth], tiles)

                def layer_norm(nth, s_at, sp_at, gain, bias):
                    mean(s_at)
                    centre(nth, sp_at, X)
                    deviation(nth)
                    dve.wait_ge(spread_ready, SP2 + SP_ALL * L + sp_at + 2)
                    scaled, last = [], []
                    for k in range(KD + 1):
                        if k < KD:
                            scaled.append(order(dve.tensor_tensor(X[:, k, 0:n_tok], X[:, k, 0:n_tok], ps[:, 5, 0:n_tok], ALU.mult)))
                        if k:
                            order.wait(scaled[k - 1])
                            last.append(order(dve.tensor_scalar(X[:, k - 1, 0:n_tok], X[:, k - 1, 0:n_tok], v2(L, gain, k - 1), v2(L, bias, k - 1),
                                                                ALU.mult, ALU.add)))
                    return lambda k: last[k]

                def add_gated(j, step, c0, m):
                    for c in range(KD + 1):
                        if c < KD:
                            v = chunk(L, j + c // 2 * step, c0 + c, n_tok)
                            for s in range(S):
                                ins = dve.scalar_tensor_tensor(out=X[:, c, lo_(s):hi_(s)], in0=v[:, lo_(s):hi_(s)], scalar=mod(L, m, c, s),
                                                               in1=X[:, c, lo_(s):hi_(s)], op0=ALU.mult, op1=ALU.add)
                            ins.then_inc(drained[c % BANKS], 1)
                        if c >= 2:
                            for k in (c - 2, c - 1):
                                dve.wait_ge(drained[k % BANKS], out_of2(L, c0 + k))
                            if c > 2:
                                order.wait()
                            ins = dve.tensor_tensor(total[:, 0:n_tok], total[:, 0:n_tok] if c > 2 else X[:, 0, 0:n_tok], X[:, c - 1, 0:n_tok], ALU.add)
                            if c < KD:
                                order(ins)
                            else:
                                ins.then_inc(total_ready, 1)

                def pool_branch(first, end):
                    add_branch(1, C2_G2, lambda c: pbuf[:, c, 0:S, PPAD:PPAD + SEQ], first, end)

                mean(S_CONV)
                pool_branch(0, 2)
                centre(0, 10, co[L])
                pool_branch(2, 4)
                deviation(0)
                pool_branch(4, 6)
                dve.wait_ge(spread_ready, SP2 + SP_ALL * L + 10 + 2)
                for k in range(KD):
                    dve.tensor_tensor(co[L][:, k, 0:n_tok], co[L][:, k, 0:n_tok], ps[:, 5, 0:n_tok], ALU.mult).then_inc(lnorm_ready, 1)
                pool_branch(6, 8)
                add_branch(2, C2_G1, lambda c: cbuf[:, c, 0:S, CPAD:CPAD + SEQ])
                if L == 0:
                    for k in range(KD):
                        rest(1, k, qk)
                add_gated(P2_OUT, 1, C2_OUT, 2)
                step = layer_norm(1, S_LN1, 12, "l1g", "l1b")
                modulate(S, 3, 2, step)
                dve.wait_ge(h2_ready, 2 * KD * L + 2 * KD)
                if L == 0:
                    dve.wait_ge(hlo_ready, 3 * KD)
                order(dve.memset(abuf[:, :, :, 0:1], 0.0))
                order(dve.memset(abuf[:, :, :, 1 + SEQ:2 + SEQ], 0.0))
                order(dve.tensor_scalar(X[:, :, 0:n_tok], X[:, :, 0:n_tok], ALPHA, None, ALU.mult))
                order.wait()
                with dve.Fori(0, KF // 2) as i:
                    order.enter(i, 4)
                    step = {}
                    for j in range(3):
                        for c in range(2):
                            src, acc = abuf[:, c, 0:S, j:j + SEQ], streams(sg[:, c, 0:n_tok], L)
                            w = v2(L, "fw", 2 * i + (j * KF + c))
                            if j == 0:
                                dve.wait_ge(drained[c], i + out_of2(L, C2_FFN + c))
                                dve.wait_ge(drained[2 + c], i + out_of2(L, C2_FFN - BANKS + 2 + c))
                                step[c] = order(dve.tensor_scalar(acc, src, w, v2(L, "fb", 2 * i + c), ALU.mult, ALU.add))
                            else:
                                order.wait(step[c])
                                ins = dve.scalar_tensor_tensor(out=acc, in0=src, scalar=w, in1=acc, op0=ALU.mult, op1=ALU.add)
                                if j == 1:
                                    step[c] = order(ins)
                                else:
                                    ins.then_inc(aconv_ready, 1)
                    for c in range(2):
                        dve.wait_ge(asilu_ready, 2 * i + (2 * (KF // 2) * L + c + 1))
                        dve.wait_ge(panels_done, 2 * i + done2(L, P2_FFN + 1))
                        dve.tensor_tensor(flat(hid2[:, bass.ds(2 * i + c, 1), 0:n_tok]), sg[:, c, 0:n_tok], ps[:, 2 + c, 0:n_tok],
                                          ALU.mult).then_inc(drained[2 + c], 1)
                    order.leave(KF // 2)
                add_gated(P2_DOWN + 2, 3, C2_DOWN, 5)
                step = layer_norm(2, S_LN2, 14, "l2g", "l2b")
                if L == DEPTH - 1:
                    order.wait()
                    dve.sem_inc(x2_ready, 1)

        def pe_second(pe, sums, spread, panel):
            for L in range(DEPTH):
                n_tok = width(L)
                tiles = n_tok // P
                a_p = P2_AT + L * P2_ALL

                def panel2(j, c, rhs, n=n_tok, turn=0, turn_c=0, **more):
                    panel(a_p + j, turn * (16 * (6 // SLOTS)) + 16 * ((a_p + j) // SLOTS + 1), [turn_c + out_of2(L, c + m - BANKS) for m in range(2)], c,
                          lambda k: rhs[:, k, 0:n], n, **more)

                def split_panel(j, c, turn=0, turn_c=0, ready=None):
                    q = NTH[j]
                    for n in range(2):
                        b = (c + n) % BANKS
                        pe.wait_ge(split_done, 12 * turn + (2 * q + n + 1))
                        pe.wait_ge(drained[b], turn_c + out_of2(L, c + n - BANKS))
                        for k in range(KD):
                            if ready and n == 0:
                                pe.wait_ge(ready[0], ready[1] + k + 1)
                            passes = ((Whi, Hhi), (Whi, Hlo), (Wlo, Hhi))
                            for m, (w, h) in enumerate(passes):
                                last = pe.matmul(ps[:, b, 0:TOK], w[:, n, k, :], h[:, k, :], start=(k == 0 and m == 0),
                                                 stop=(k == KD - 1 and m == len(passes) - 1))
                        last.then_inc((halves_done, panels_done)[n], 1)

                INPUTS = ((h2_ready, 2 * KD * L), (gated, 24 * L + 16), (h2_ready, 2 * KD * L + KD))

                def from_h(j, c, n=n_tok, nth_input=None, rhs=Hn, **more):
                    if nth_input is not None:
                        more["ready"] = INPUTS[nth_input] if L else (hlo_ready, KD * nth_input)
                    if L == 0:
                        split_panel(j, c, **more)
                    else:
                        panel2(j, c, rhs, n, **more)

                def four(j, c):
                    for m in range(4):
                        from_h(j + m, c + 2 * m)

                def mean(s_at, nth):
                    pe.wait_ge(total_ready, 3 * L + nth + 1)
                    sums([[total[:, t * P:(t + 1) * P]] for t in range(tiles)], T("inv_d"))

                def spread_norm(bank, s_at):
                    pe.wait_ge(scale_ready, SUM2 + S_ALL * L + s_at + 1)
                    spread(bank, 0, tiles)

                def variance(nth):
                    for k in range(PAIRS):
                        pe.wait_ge(pairs_ready, (3 * L + nth) * PAIRS + k + 1)
                        for t in range(tiles):
                            last = pe.matmul(ps[:, 7, t:t + 1], pooled[:, 2 * k, t * P:(t + 1) * P], T("inv_d"),
                                             start=(k == 0 and t == 0), stop=(k == PAIRS - 1 and t == tiles - 1))
                    last.then_inc(sums_ready, 1)

                def layer_norm(s_at, nth):
                    mean(s_at, nth)
                    spread_norm(4, s_at)
                    variance(nth)
                    spread_norm(5, s_at + 1)

                for j in range(8):
                    from_h(P2_CONV + j, C2_CONV + 2 * j, nth_input=0 if j == 0 else None)
                for j in range(6):
                    from_h(P2_QKV + j, C2_QKV + 2 * j, n_tok if j < 4 else TOK)
                four(P2_POOL, C2_POOL)
                pe.wait_ge(drained[3], out_of2(L, C2_QKV + 11))
                for t in range(4):
                    for v in range(KV_HEADS):
                        e = KV_HEADS * t + v
                        last = pe.transpose(ps[:, 4 + e // 4, e % 4 * P:(e % 4 + 1) * P], vT[:, v, t * P:(t + 1) * P], ident)
                last.then_inc(v_turned, 1)
                pe.wait_ge(squares_ready, SQ2 + SQ_ALL * L + 2)
                cells = qk_tiles(L)
                sums([[(pooled[:, c, :] if c < N_HEADS else ksq[:, c - N_HEADS, :])[:, t * P:(t + 1) * P]] for c, t in cells], T("inv_p"))
                pe.wait_ge(scale_ready, SUM2 + S_ALL * L + S_QK + 1)
                pe.wait_ge(v_ready, L + 1)

                def norm_spread(c):
                    spread(4 + c % 3, cells.index((c, 0)), sum(m == c for m, _ in cells))

                for c in range(3):
                    norm_spread(c)
                for c in range(10):
                    pe.wait_ge(rotated, 10 * L + c + 1)
                    pe.matmul(ps[:, 4 + c % 3, 0:SEQ], T("perm"), qk[:, c, 0:SEQ], start=True, stop=True).then_inc(perm_ready, 1)
                    if c + 3 < 10:
                        pe.wait_ge(rope_done, 10 * L + c + 1)
                        norm_spread(c + 3)
                pe.wait_ge(rope_done, 10 * L + 10)
                for b in (2, 3):
                    pe.wait_ge(drained[b], out_of2(L, C2_POOL + 4 + b))
                todo, a0 = items(L), items_before(L)

                def score(i):
                    h, t, k0, n = todo[i]
                    if i >= 2:
                        pe.wait_ge(exp_ready, a0 + i - 1)
                    pe.matmul(ps[:, 4 + i % 2, 0:n], qk[:, h, t * P:(t + 1) * P], qk[:, N_HEADS + h // (N_HEADS // KV_HEADS), k0:k0 + n],
                              start=True, stop=True).then_inc(score_mm, 1)

                score(0)
                score(1)
                def output(i):
                    h, t, k0, n = todo[i]
                    kv = h // (N_HEADS // KV_HEADS)
                    pe.wait_ge(probT_ready, a0 + i + 1)
                    if i >= 2:
                        pe.wait_ge(attn_ready, a0 + i - 1)
                    for m in range(n // P):
                        last = pe.matmul(ps[:, O_BANKS[i % 2], 0:P], vt2[:, k0 // P + m, kv * P:(kv + 1) * P], probT[:, i % 2, m * P:(m + 1) * P],
                                         start=(m == 0), stop=(m == n // P - 1))
                    last.then_inc(o_mm, 1)

                for i, (_, _, _, n) in enumerate(todo):
                    pe.wait_ge(prob_ready, a0 + i + 1)
                    if i >= 2:
                        pe.wait_ge(probT_ready, a0 + i - 1)
                    for m in range(n // P):
                        last = pe.transpose(ps[:, T_BANKS[i % 2], m * P:(m + 1) * P], prob[:, i % 2, m * P:(m + 1) * P], ident)
                    last.then_inc(turn_mm, 1)
                    if i + 2 < len(todo):
                        score(i + 2)
                    if i:
                        output(i - 1)
                output(len(todo) - 1)
                pe.wait_ge(attn_ready, a0 + len(todo))
                four(P2_G0, C2_G0)
                pe.wait_ge(pooled_ready, KD * (L + 1))
                for j in range(4):
                    panel2(P2_PMIX + j, C2_PMIX + 2 * j, pooled[:, 2 * j:2 * j + 2, :], part=(0, 2), k_all=2)
                from_h(P2_G2, C2_G2)
                mean(S_CONV, 0)
                spread_norm(4, S_CONV)
                from_h(P2_G2 + 1, C2_G2 + 2)
                variance(0)
                from_h(P2_G2 + 2, C2_G2 + 4)
                spread_norm(5, S_CONV + 1)
                from_h(P2_G2 + 3, C2_G2 + 6)
                for m in range(4):
                    panel2(P2_PW + m, C2_PW + 2 * m, co[L], ready=(lsilu_ready, KD * L) if m == 0 else None)
                four(P2_G1, C2_G1)
                for m in range(4):
                    from_h(P2_OUT + m, C2_OUT + 2 * m, rhs=qk, nth_input=1 if m == 0 else None)
                layer_norm(S_LN1, 1)
                with pe.Fori(0, 3) as i:
                    for j in range(6):
                        from_h(P2_FFN + j, C2_FFN + 2 * j, turn=i, turn_c=3 * i, nth_input=2 if j == 0 else None)
                for j in range(18, 22):
                    from_h(P2_FFN + j, C2_FFN + 2 * j)
                with pe.Fori(0, 2) as i:
                    pe.wait_ge(drained[3], out_of2(L, C2_FFN + 43))
                    for j in range(6):
                        panel2(P2_DOWN + j, C2_DOWN + j // 3 * 2, hid2, turn=i, turn_c=i, part=KPARTS[j % 3], k_all=KF)
                layer_norm(S_LN2, 2)

        @block.sync
        def _(sp):
            sp.dma_start(X1, x).then_inc(loaded, 16)
            sp.dma_start(tab[:, :], tabs).then_inc(loaded, 16)
            sp.sem_inc(panels_done, SLOTS)
            for b in range(BANKS):
                sp.sem_inc(drained[b], 1)

            def load(panel, j, src, waited=False, split=None):
                s = j % SLOTS
                if split is not None:
                    sp.wait_ge(split_done, 2 * split + 2)
                elif not waited:
                    sp.wait_ge(panels_done, panel + 1)
                sp.dma_start(W[:, s, 0:src.shape[1], 0:src.shape[2]], src).then_inc(panel_loaded[s], 16)

            with sp.Fori(0, DEPTH) as l:
                at_ = l * P1_ALL
                wi = rows(w_in[l])
                for j in range(2):
                    load(at_ + (P1_BA + j), P1_BA + j, wi[:, 4 * j:4 * j + 4, B_AT:B_AT + NE])
                sp.wait_ge(panels_done, at_ + (P1_QKV + 1))
                sp.sem_inc(layer_opened, 1)
                load(at_ + P1_QKV, P1_QKV, wi[:, :, 0:PC], waited=True)
                for j in range(1, 8):
                    load(at_ + (P1_QKV + j), P1_QKV + j, wi[:, :, j * PC:(j + 1) * PC])
                for j, part in enumerate((1, 1, 2, 2, 0, 0)):
                    c = SC_AT + 512 * part + PC * (j % 2)
                    load(at_ + (P1_GC + j), P1_GC + j, wi[:, :, c:c + PC])
                with sp.Fori(0, 4) as i:
                    for j in range(6):
                        load(at_ + (P1_ADA + j) + 6 * i, P1_ADA + j, rows(w_ada[l])[:, :, bass.ds((6 * i + j) * PC, PC)])
                for j in range(4):
                    load(at_ + (P1_OUT + j), P1_OUT + j, rows(w_out[l])[:, :, j * PC:(j + 1) * PC])
                with sp.Fori(0, 3) as i:
                    for j in range(6):
                        w = rows((w_gate, w_up)[j % 2][l])
                        load(at_ + (P1_FFN + j) + 6 * i, P1_FFN + j, w[:, :, bass.ds((3 * i + j // 2) * PC, PC)])
                for j in range(18, 22):
                    w = rows((w_gate, w_up)[j % 2][l])
                    load(at_ + (P1_FFN + j), P1_FFN + j, w[:, :, j // 2 * PC:(j // 2 + 1) * PC])
                with sp.Fori(0, 2) as i:
                    for j in range(6):
                        w = rows(w_down[l], *KPARTS[j % 3])
                        load(at_ + (P1_DOWN + j) + 6 * i, P1_DOWN + j, w[:, :, bass.ds((2 * i + j // 3) * PC, PC)])
            load_second(sp, load)
            sp.dma_start(out, X1).then_inc(stored, 16)
            sp.wait_ge(stored, 16)

        @block.gpsimd
        def _(pool):
            pool.dma_start(cnd, cond).then_inc(cond_loaded, 16)
            pool.dma_start(pf[:, :], vec_final).then_inc(vec2_loaded, 16)
            pool.dma_start(p2[:, :], vec2).then_inc(vec2_loaded, 16)
            with pool.Fori(0, DEPTH) as l:
                pool.wait_ge(drained[3], out_of(l, -1))
                pool.dma_start(p1[:, :], vec1[l]).then_inc(vec1_loaded, 16)
                pool.wait_ge(at_ready, l + 1)
                for s in range(LEVELS):
                    if s >= 2:
                        pool.wait_ge(inv_m, l * LEVELS + (s - 1))
                    pool.tensor_tensor(Bt[:, s % 2, :].rearrange("p (e c) -> p e c", e=NE), AT,
                                       T("level", s * P, P).unsqueeze(1).to_broadcast([P, NE, P]),
                                       ALU.mult).then_inc(blocks_ready, 1)
            pool_second(pool)

        @block.scalar
        def _(act):
            order = Order(act, act_order)
            act.wait_ge(loaded, 32)
            for k in range(KD):
                act.activation(sq1[:, k, :], X1[:, k, :], ACT.Square).then_inc(squares_ready, 1)

            def squares(dst, src):
                act.activation(dst, src, ACT.Square).then_inc(squares_ready, 1)

            def root(nth, n, eps="eps"):
                act.wait_ge(sums_ready, nth[0] + 1)
                act.activation(roots[:, 0:n], ps[:, 7, 0:n], ACT.Sqrt, bias=T(eps)).then_inc(root_ready, 1)

            def evacuate(l, j, c, dst, func=ACT.Copy):
                act.wait_ge(panels_done, done(l, j))
                act.activation(dst, ps[:, c % BANKS, 0:SEQ], func).then_inc(drained[c % BANKS], 1)

            def ada(l, jj):
                act.wait_ge(panels_done, done(l, P1_ADA + jj))
                if jj >= 12:
                    act.wait_ge(ada_turned, N_ADA * l + (jj - 11))
                act.activation(ada_rows(jj), ps[0:2, jj % ADA_BANKS, 0:PC], ACT.Copy).then_inc(ada_out, 1)

            act.wait_ge(cond_loaded, 16)
            act.activation(cnd, cnd, ACT.Silu).then_inc(cond_ready, 1)
            with act.Fori(0, DEPTH) as l:
                order.enter(l, 5)
                norm = l * N1_ALL
                root([norm + N1_IN], 2)
                act.wait_ge(vec1_loaded, 16 * l + 16)
                act.wait_ge(gin_ready, l + 1)
                act.activation(beta.rearrange("p (n h) -> p n h", n=2), ps[:, 6, 0:2 * NE].rearrange("p (n h) -> p n h", n=2)[:, :, 0:HEADS],
                               ACT.Sigmoid).then_inc(beta_ready, 1)
                order(act.activation(gabs, gin, ACT.Abs))
                order.wait()
                order(act.activation(gexp, gabs, ACT.Exp, scale=-1.0))
                order(act.activation(rates, v1("alog", 0, HEADS), ACT.Exp))
                order.wait()
                act.activation(gsp, gexp, ACT.Ln, bias=T("one")).then_inc(log_ready, 1)
                for c in range(14):
                    if c < 12:
                        evacuate(l, P1_QKV + c // 2, C1_QKV + c, xpad[:, c, CONV - 1:])
                    if c >= 2:
                        act.wait_ge(conv1_ready, 12 * l + (c - 1))
                        act.activation(qkv[:, c - 2, :], qkv[:, c - 2, :], ACT.Silu).then_inc(silu_ready, 1)
                for c in range(4):
                    evacuate(l, P1_Z + c // 2, C1_Z + c, zs[:, c, :], ACT.Silu)
                act.wait_ge(silu_ready, 12 * l + 8)
                for k in range(2):
                    squares(sq1[:, 4 * k:4 * k + 4, :], qkv[:, 4 * k:4 * k + 4, :])
                root([norm + N1_L2], 16)
                for c in range(4):
                    evacuate(l, P1_GC + c // 2, C1_GC + c, gc[:, c, :])
                act.wait_ge(turned, 2 * l + 1)
                act.activation(flat(ktok), flat(ps[:, 4:6, :]), ACT.Copy).then_inc(ktok_ready, 1)
                for c in range(4):
                    evacuate(l, P1_GB + c // 2, C1_GB + c, gb[:, c, :])
                act.wait_ge(diff_ready, l + 1)
                act.activation(flat(DT), flat(DT), ACT.Exp).then_inc(decay_ready, 1)
                act.activation(egc, gcol, ACT.Exp)
                act.activation(flat(qdec), ps[:, 5, :], ACT.Exp).then_inc(exps_ready, 1)
                for jj in range(7):
                    ada(l, jj)
                for s in range(1, LEVELS):
                    act.wait_ge(inv_mm, l * (2 * LEVELS - 1) + 2 * s)
                    act.activation(flat(Y), flat(ps[:, 4:6, :]), ACT.Copy).then_inc(inv_y, 1)
                    for jj in range(2):
                        ada(l, 5 + 2 * s + jj)
                act.wait_ge(scan_mm, 6 * l + 1)
                act.activation(flat(u0), ps[:, 4, :], ACT.Copy).then_inc(scan_in, 1)
                act.wait_ge(scan_mm, 6 * l + 2)
                act.activation(flat(nw), ps[:, 5, :], ACT.Copy, scale=-1.0).then_inc(scan_in, 1)
                ada(l, 19)
                act.wait_ge(scan_mm, 6 * l + 3)
                act.activation(flat(S1), ps[:, 6, :], ACT.Copy).then_inc(scan_in, 1)
                act.wait_ge(scan_mm, 6 * l + 4)
                order(act.activation(odn[:, :, 0:P], ps[:, 7, :].rearrange("p (h c) -> p h c", h=HEADS), ACT.Copy))
                ada(l, 20)
                act.wait_ge(scan_mm, 6 * l + 5)
                act.activation(flat(vnew), ps[:, 4, :], ACT.Copy).then_inc(scan_in, 1)
                ada(l, 21)
                act.wait_ge(scan_mm, 6 * l + 6)
                order(act.activation(odn[:, :, P:SEQ], ps[:, 5, :].rearrange("p (h c) -> p h c", h=HEADS), ACT.Copy))
                act.wait_ge(y_ready, HEADS * l + HEADS)
                squares(sq1[:, 4:8, :], ysc)
                order.wait()
                squares(sq1[:, 0:4, :], odn)
                for jj in range(22, N_ADA):
                    ada(l, jj)
                root([norm + N1_MIX], 16)
                for c in range(KD):
                    act.wait_ge(drained[c % BANKS], out_of(l, C1_OUT + c))
                    squares(sq1[:, c, :], X1[:, c, :])
                root([norm + N1_FFN], 2)
                with act.Fori(0, KF // 2) as i:
                    for c in range(2):
                        act.wait_ge(panels_done, done(l, P1_FFN) + 2 * i)
                        act.wait_ge(drained[2 + c], out_of(l, C1_FFN - BANKS + 2 + c) + i)
                        act.activation(gs1[:, c, :], ps[:, c, 0:SEQ], ACT.Silu).then_inc(drained[c], 1)
                for c in range(KD):
                    act.wait_ge(drained[c % BANKS], out_of(l, C1_DOWN + c))
                    squares(sq1[:, c, :], X1[:, c, :])
                order.leave(DEPTH)
            root([N_FINAL], 2)
            act.wait_ge(vec2_loaded, 32)
            act_second(act, order, squares, root)

        @block.vector
        def _(dve):
            order = Order(dve, dve_order)

            def invert(nth, n):
                dve.wait_ge(root_ready, nth[0] + 1)
                dve.reciprocal(scales[:, 0:n], roots[:, 0:n]).then_inc(scale_ready, 1)

            def chunk(l, j, c):
                dve.wait_ge(panels_done, done(l, j))
                return ps[:, c % BANKS, 0:SEQ]

            def normalise(norm, spreads, gain, dst):
                invert([norm], 2)
                dve.wait_ge(spread_ready, spreads)
                for k in range(KD):
                    dve.scalar_tensor_tensor(out=dst[:, k, :], in0=X1[:, k, :], scalar=gain(k), in1=ps[:, 4, 0:SEQ],
                                             op0=ALU.mult, op1=ALU.mult).then_inc(h_ready, 1)

            def tiles(v):
                return v.rearrange("p (n h) -> p n h", n=2)

            def add_square(c, squares):
                dve.wait_ge(squares_ready, squares)
                if c > 1:
                    order.wait()
                ins = dve.tensor_tensor(sq1[:, 0, :], sq1[:, 0, :], sq1[:, c, :], ALU.add)
                if c < KD - 1:
                    order(ins)
                else:
                    ins.then_inc(square_sum_ready, 1)

            def residual(l, j, step, c0, squares):
                for c in range(KD + 1):
                    if c < KD:
                        v = chunk(l, j + c // 2 * step, c0 + c)
                        dve.tensor_tensor(X1[:, c, :], X1[:, c, :], v, ALU.add).then_inc(drained[c % BANKS], 1)
                    if c > 1:
                        add_square(c - 1, squares + c)

            dve.memset(xpad[:, :, 0:CONV - 1], 0.0)
            dve.memset(spad[:, :, 0:SC_CONV - 1], 0.0)
            dve.wait_ge(loaded, 32)
            for c in range(1, KD):
                add_square(c, c + 1)
            with dve.Fori(0, DEPTH) as l:
                order.enter(l, 79)
                norm = l * N1_ALL
                dve.wait_ge(vec1_loaded, 16 * l + 16)
                normalise(norm + N1_IN, l * 6 + 1, lambda k: v1("norm1", k), H1)
                dve.wait_ge(panels_done, done(l, P1_BA + 1))
                dve.tensor_copy(ba_rows, ps[0:NE, 5, 0:SEQ]).then_inc(ba_out, 1)
                dve.wait_ge(ba_turned, l + 1)
                dve.tensor_tensor(tiles(gin), tiles(ps[:, 6, 0:2 * NE])[:, :, HEADS:NE],
                                  v1("dtb", 0, HEADS).unsqueeze(1).to_broadcast([P, 2, HEADS]), ALU.add).then_inc(gin_ready, 1)
                dve.wait_ge(log_ready, l + 1)
                order(dve.scalar_tensor_tensor(out=gmax, in0=gin, scalar=0.0, in1=gsp, op0=ALU.max, op1=ALU.add))
                order.wait()
                dve.scalar_tensor_tensor(out=tiles(glog), in0=tiles(gmax), scalar=-1.0,
                                         in1=rates.unsqueeze(1).to_broadcast([P, 2, HEADS]),
                                         op0=ALU.mult, op1=ALU.mult).then_inc(g_ready, 1)
                for c0 in range(0, 12, 2):
                    step = {}
                    for j in range(CONV):
                        for c in range(c0, c0 + 2):
                            w = v1("dnw", j * 12 + c)
                            src = xpad[:, c, j:j + SEQ]
                            if j == 0:
                                dve.wait_ge(drained[c % BANKS], out_of(l, C1_QKV + c))
                                step[c] = order(dve.tensor_scalar(qkv[:, c, :], src, w, None, ALU.mult))
                            else:
                                order.wait(step[c])
                                ins = dve.scalar_tensor_tensor(out=qkv[:, c, :], in0=src, scalar=w, in1=qkv[:, c, :],
                                                               op0=ALU.mult, op1=ALU.add)
                                if j < CONV - 1:
                                    step[c] = order(ins)
                                else:
                                    ins.then_inc(conv1_ready, 1)
                invert([norm + N1_L2], 16)
                for i in range(2):
                    dve.wait_ge(spread_ready, l * 6 + 2 + i)
                    v = flat(qkv[:, 4 * i:4 * i + 4, :])
                    dve.scalar_tensor_tensor(out=v, in0=v, scalar=P ** -0.5 if i == 0 else 1.0, in1=flat(ps[:, 4 + 2 * i:6 + 2 * i, :]),
                                             op0=ALU.mult, op1=ALU.mult).then_inc(qk_ready, 1)
                for c in range(4):
                    dve.wait_ge(drained[c], out_of(l, C1_GC + c))
                    dve.tensor_tensor(spad[:, c, SC_CONV - 1:], chunk(l, P1_HV + c // 2, C1_HV + c), gc[:, c, :], ALU.mult).then_inc(drained[c], 1)
                dve.wait_ge(turned, 2 * l + 2)
                dve.wait_ge(beta_ready, l + 1)
                dve.tensor_tensor(vtok, flat(ps[:, 6:8, :]).rearrange("p (e c) -> p e c", e=NE),
                                  beta.unsqueeze(2).to_broadcast([P, NE, P]), ALU.mult).then_inc(vtok_ready, 1)
                dve.wait_ge(cum_ready, 2 * l + 1)
                order(dve.tensor_copy(gcol, ps[:, 6, 0:NE]))
                order.wait()
                dve.wait_ge(cum_ready, 2 * l + 2)
                for e in range(NE):
                    ins = dve.scalar_tensor_tensor(out=DT[:, e, :], in0=ps[:, 4 + e // 4, e % 4 * P:(e % 4 + 1) * P],
                                                   scalar=gcol[:, e:e + 1], in1=T("cap"), op0=ALU.subtract, op1=ALU.min)
                ins.then_inc(diff_ready, 1)
                dve.wait_ge(decay_ready, l + 1)
                dve.wait_ge(kk_ready, 3 * l + 1)
                dve.tensor_tensor(flat(AT), flat(ps[:, 6:8, :]), flat(DT), ALU.mult).then_inc(kk_used, 1)
                dve.wait_ge(kk_used, l + 1)
                dve.wait_ge(kk_ready, 3 * l + 2)
                dve.tensor_tensor(flat(AT), flat(ps[:, 4:6, :]), flat(AT), ALU.mult).then_inc(at_ready, 1)
                dve.wait_ge(kk_ready, 3 * l + 3)
                dve.tensor_tensor(flat(qkT), flat(ps[:, 6:8, :]), flat(DT), ALU.mult)
                dve.wait_ge(drained[3], out_of(l, C1_HV + 3))
                for j in range(SC_CONV):
                    for c in range(4):
                        w = v1("scw", j * 4 + c)
                        src = spad[:, c, j:j + SEQ]
                        if j == 0:
                            order(dve.tensor_scalar(ysc[:, c, :], src, w, None, ALU.mult))
                        else:
                            order(dve.scalar_tensor_tensor(out=ysc[:, c, :], in0=src, scalar=w, in1=ysc[:, c, :],
                                                           op0=ALU.mult, op1=ALU.add))
                    order.wait()
                for c in range(4):
                    dve.wait_ge(drained[c], out_of(l, C1_GB + c))
                    dve.tensor_tensor(ysc[:, c, :], ysc[:, c, :], gb[:, c, :], ALU.mult).then_inc(y_ready, 1)
                dve.wait_ge(blocks_ready, l * LEVELS + 1)
                dve.scalar_tensor_tensor(out=MT, in0=Bt[:, 0, :].rearrange("p (e c) -> p e c", e=NE), scalar=-1.0,
                                         in1=ident.unsqueeze(1).to_broadcast([P, NE, P]),
                                         op0=ALU.mult, op1=ALU.add).then_inc(inv_m, 1)
                dve.wait_ge(inv_mm, l * (2 * LEVELS - 1) + 1)
                dve.tensor_copy(flat(M), flat(ps[:, 4:6, :])).then_inc(inv_turned, 1)
                dve.wait_ge(exps_ready, l + 1)
                order(dve.tensor_tensor(bge, beta, egc, ALU.mult))
                order.wait()
                for h in range(HEADS):
                    order(dve.tensor_scalar(kbg[:, h, :], ktok[:, HEADS + h, :], bge[:, HEADS + h:HEADS + h + 1], None, ALU.mult))
                    order(dve.tensor_scalar(kdec[:, h, :], ktok[:, h, :], DT[:, h, P - 1:P], None, ALU.mult))
                dve.tensor_tensor(qdec, qdec, qkv[:, 0:HEADS, P:SEQ], ALU.mult).then_inc(keys_ready, 1)
                for s in range(1, LEVELS):
                    dve.wait_ge(inv_mm, l * (2 * LEVELS - 1) + (2 * s + 1))
                    if s < LEVELS - 1:
                        if s == 1:
                            dve.wait_ge(inv_turned, l + 1)
                        else:
                            dve.wait_ge(inv_m, l * LEVELS + s)
                        dve.tensor_tensor(flat(M), flat(M), flat(ps[:, 6:8, :]), ALU.subtract)
                    dve.tensor_tensor(flat(MT), flat(MT), flat(ps[:, 4:6, :]), ALU.subtract).then_inc(inv_m, 1)
                invert([norm + N1_MIX], 16)
                dve.wait_ge(ada_turned, N_ADA * l + N_ADA)
                dve.tensor_tensor(mods[:, bass.ds(l * (N_MOD * KD * 2), N_MOD * KD * 2)].rearrange("p (k c) -> p k c", c=2),
                                  ps[:, 3, 0:N_MOD * KD * 2].rearrange("p (k c) -> p k c", c=2),
                                  v1("ada", 0, N_MOD * KD).unsqueeze(2).to_broadcast([P, N_MOD * KD, 2]),
                                  ALU.add).then_inc(mods_ready, 1)
                for i in range(2):
                    dve.wait_ge(spread_ready, l * 6 + 4 + i)
                    for h in range(HEADS):
                        ins = dve.scalar_tensor_tensor(out=mix1[:, 4 * i + h, :], in0=(odn, ysc)[i][:, h, :],
                                                       scalar=v1("dng") if i == 0 else v1("scg", h),
                                                       in1=ps[:, 4 + 2 * i + h // 2, h % 2 * SEQ:(h % 2 + 1) * SEQ],
                                                       op0=ALU.mult, op1=ALU.mult)
                        order(ins)
                order.wait()
                dve.wait_ge(drained[3], out_of(l, C1_Z + 3))
                dve.tensor_tensor(mix1[:, 0:4, :], mix1[:, 0:4, :], zs, ALU.mult).then_inc(mix_ready, 1)
                residual(l, P1_OUT, 1, C1_OUT, SQ1_ALL * l + 12)
                normalise(norm + N1_FFN, l * 6 + 6, lambda k: v1("norm2", k), H1)
                with dve.Fori(0, KF // 2) as i:
                    for c in range(2):
                        dve.wait_ge(drained[c], out_of(l, C1_FFN + c) + i)
                        dve.wait_ge(panels_done, done(l, P1_FFN + 1) + 2 * i)
                        dve.tensor_tensor(hid1[:, bass.ds(2 * i + c, 1), :].rearrange("p a t -> p (a t)"), gs1[:, c, :],
                                          ps[:, 2 + c, 0:SEQ], ALU.mult).then_inc(drained[2 + c], 1)
                residual(l, P1_DOWN + 2, 3, C1_DOWN, SQ1_ALL * l + 20)
                order.leave(DEPTH)
            dve.wait_ge(vec2_loaded, 32)
            prepare_modulation(dve, order)
            normalise(N_FINAL, 6 * DEPTH + 1, lambda k: pf[:, k:k + 1], X1)
            dve_second(dve, order, invert)

        @block.tensor
        def _(pe):
            def sums(lhs, weight):
                for i, parts in enumerate(lhs):
                    for n, part in enumerate(parts):
                        last = pe.matmul(ps[:, 7, i:i + 1], part, weight, start=(n == 0), stop=(n == len(parts) - 1))
                last.then_inc(sums_ready, 1)

            def spread(bank, first, n):
                for i in range(n):
                    last = pe.matmul(ps[:, bank + i // 4, i % 4 * P:(i % 4 + 1) * P],
                                     scales[:, first + i:first + i + 1].to_broadcast([P, P]), ident, start=True, stop=True)
                last.then_inc(spread_ready, 1)

            def norm_of_x(norm, summed):
                pe.wait_ge(square_sum_ready, summed)
                sums([[sq1[:, 0, t * P:(t + 1) * P]] for t in range(2)], T("inv_d"))
                pe.wait_ge(scale_ready, norm + 1)
                spread(4, 0, 2)

            def panel(j, loads, frees, c, rhs, n_tok, part=(0, KD), k_all=KD, ready=None):
                s = j % SLOTS
                k0, kn = part
                pe.wait_ge(panel_loaded[s], loads)
                for n in range(2):
                    b = (c + n) % BANKS
                    if k0 == 0:
                        pe.wait_ge(drained[b], frees[n])
                    for k in range(kn):
                        if ready and n == 0:
                            pe.wait_ge(ready[0], ready[1] + k + 1)
                        last = pe.matmul(ps[:, b, 0:n_tok], W[:, s, k, n * P:(n + 1) * P], rhs(k0 + k),
                                         start=(k0 + k == 0), stop=(k0 + k == k_all - 1))
                last.then_inc(panels_done, 1)

            def loads1(l, j):
                return l * (16 * P1_ALL // SLOTS) + 16 * (j // SLOTS + 1)

            def panel1(l, j, c, rhs, turn=0, **more):
                turn_c = more.pop("turn_c", 0)
                panel(j, loads1(l, j) + 16 * (6 // SLOTS) * turn, [out_of(l, c + n - BANKS) + turn_c for n in range(2)], c,
                      lambda k: rhs[:, k, 0:SEQ], SEQ, **more)

            def problems(bank, lhs, rhs):
                for e in range(NE):
                    last = pe.matmul(ps[:, bank + e // 4, e % 4 * P:(e % 4 + 1) * P], lhs(e), rhs(e), start=True, stop=True)
                return last

            def heads(bank, *products):
                for h in range(HEADS):
                    for n, (lhs, rhs) in enumerate(products):
                        last = pe.matmul(ps[:, bank, h * P:(h + 1) * P], lhs(h), rhs(h), start=(n == 0), stop=(n == len(products) - 1))
                return last

            def ada_columns(l, jj):
                for n in range(2):
                    c = 2 * (2 * jj + n)
                    last = pe.matmul(ps[:, 3, c:c + 2], ada_rows(jj)[:, n * P:(n + 1) * P], ident[0:2, 0:2], start=True, stop=True)
                last.then_inc(ada_turned, 1)

            def ada(l, jj):
                j = P1_ADA + jj
                s = j % SLOTS
                pe.wait_ge(panel_loaded[s], loads1(l, j))
                if jj >= ADA_BANKS:
                    pe.wait_ge(ada_out, N_ADA * l + (jj - ADA_BANKS + 1))
                    ada_columns(l, jj - ADA_BANKS)
                for k in range(KD):
                    last = pe.matmul(ps[0:2, jj % ADA_BANKS, 0:PC], cnd[:, k, :], W[:, s, k, :], start=(k == 0), stop=(k == KD - 1))
                last.then_inc(panels_done, 1)

            def tile_of(v, first):
                return lambda e: v[:, first + e % HEADS, e // HEADS * P:(e // HEADS + 1) * P]

            pe.wait_ge(loaded, 32)
            pe.wait_ge(cond_ready, 1)
            with pe.Fori(0, DEPTH) as l:
                norm = l * N1_ALL
                norm_of_x(norm + N1_IN, 2 * l + 1)
                pe.wait_ge(h_ready, 16 * l + 8)
                for j in range(2):
                    pe.wait_ge(panel_loaded[P1_BA + j], loads1(l, P1_BA + j))
                    for k in range(KD // 2):
                        last = pe.matmul(ps[0:NE, 5, 0:SEQ], W[:, P1_BA + j, k, 0:NE], H1[:, KD // 2 * j + k, :],
                                         start=(j == 0 and k == 0), stop=(j == 1 and k == KD // 2 - 1))
                    last.then_inc(panels_done, 1)
                for j in range(2):
                    panel1(l, P1_QKV + j, C1_QKV + 2 * j, H1)
                pe.wait_ge(ba_out, l + 1)
                for t in range(2):
                    last = pe.matmul(ps[:, 6, NE * t:NE * (t + 1)], ba_rows[:, t * P:(t + 1) * P], ident[0:NE, 0:NE], start=True, stop=True)
                last.then_inc(ba_turned, 1)
                for j in range(2, 8):
                    panel1(l, P1_QKV + j, C1_QKV + 2 * j, H1)
                pe.wait_ge(squares_ready, SQ1_ALL * l + 10)
                sums([[sq1[:, c, t * P:(t + 1) * P]] for c in range(8) for t in range(2)], T("one"))
                for j in range(2):
                    panel1(l, P1_GC + j, C1_GC + 2 * j, H1)
                pe.wait_ge(scale_ready, norm + (N1_L2 + 1))
                spread(4, 0, 8)
                spread(6, 8, 8)
                for j in range(2):
                    panel1(l, P1_HV + j, C1_HV + 2 * j, H1)
                pe.wait_ge(qk_ready, 2 * l + 2)
                pe.wait_ge(silu_ready, 12 * l + 12)
                for bank, first in ((4, HEADS), (6, 2 * HEADS)):
                    src = tile_of(qkv, first)
                    for e in range(NE):
                        last = pe.transpose(ps[:, bank + e // 4, e % 4 * P:(e % 4 + 1) * P], src(e), ident)
                    last.then_inc(turned, 1)
                for j in range(2):
                    panel1(l, P1_GB + j, C1_GB + 2 * j, H1)
                pe.wait_ge(g_ready, l + 1)
                pe.wait_ge(vtok_ready, l + 1)
                pe.matmul(ps[:, 6, 0:NE], T("upper"), glog, start=True, stop=True).then_inc(cum_ready, 1)
                pe.wait_ge(ktok_ready, l + 1)
                problems(4, lambda e: glog[:, e:e + 1].to_broadcast([P, P]), lambda e: T("upper")).then_inc(cum_ready, 1)
                for b in range(BANKS):
                    pe.wait_ge(drained[b], out_of(l, C1_GB + b))
                for jj in range(2):
                    ada(l, jj)
                pe.wait_ge(diff_ready, l + 1)
                problems(6, tile_of(qkv, HEADS), tile_of(qkv, HEADS)).then_inc(kk_ready, 1)
                ada(l, 2)
                pe.wait_ge(exps_ready, l + 1)
                problems(4, lambda e: beta[:, e:e + 1].to_broadcast([P, P]), lambda e: ident).then_inc(kk_ready, 1)
                ada(l, 3)
                pe.wait_ge(kk_used, l + 1)
                problems(6, tile_of(qkv, HEADS), tile_of(qkv, 0)).then_inc(kk_ready, 1)
                for jj in range(4, 6):
                    ada(l, jj)
                pe.wait_ge(inv_m, l * LEVELS + 1)
                for e in range(NE):
                    last = pe.transpose(ps[:, 4 + e // 4, e % 4 * P:(e % 4 + 1) * P], MT[:, e, :], ident)
                last.then_inc(inv_mm, 1)
                ada(l, 6)
                for s in range(1, LEVELS):
                    B = Bt[:, s % 2, :].rearrange("p (e c) -> p e c", e=NE)
                    pe.wait_ge(blocks_ready, l * LEVELS + (s + 1))
                    if s == 1:
                        pe.wait_ge(inv_turned, l + 1)
                    else:
                        pe.wait_ge(inv_m, l * LEVELS + s)
                    problems(4, lambda e: B[:, e, :], lambda e: M[:, e, :]).then_inc(inv_mm, 1)
                    ada(l, 5 + 2 * s)
                    pe.wait_ge(inv_y, l * (LEVELS - 1) + s)
                    if s < LEVELS - 1:
                        problems(6, lambda e: MT[:, e, :], lambda e: Y[:, e, :])
                    problems(4, lambda e: Y[:, e, :], lambda e: MT[:, e, :]).then_inc(inv_mm, 1)
                    ada(l, 6 + 2 * s)
                pe.wait_ge(inv_m, l * LEVELS + LEVELS)
                pe.wait_ge(keys_ready, l + 1)
                second = lambda v: lambda h: v[:, HEADS + h, :]
                first = lambda v: lambda h: v[:, h, :]
                heads(4, (first(MT), first(vtok))).then_inc(scan_mm, 1)
                heads(5, (first(kbg), second(MT))).then_inc(scan_mm, 1)
                ada(l, 19)
                pe.wait_ge(scan_in, 4 * l + 1)
                heads(6, (first(kdec), first(u0))).then_inc(scan_mm, 1)
                heads(7, (first(u0), first(qkT))).then_inc(scan_mm, 1)
                ada(l, 20)
                pe.wait_ge(scan_in, 4 * l + 3)
                heads(4, (second(MT), second(vtok)), (first(nw), first(S1))).then_inc(scan_mm, 1)
                ada(l, 21)
                pe.wait_ge(scan_in, 4 * l + 4)
                heads(5, (first(S1), first(qdec)), (first(vnew), second(qkT))).then_inc(scan_mm, 1)
                for jj in range(22, N_ADA):
                    ada(l, jj)
                pe.wait_ge(squares_ready, SQ1_ALL * l + 12)
                sums([[sq1[:, c, t * P:(t + 1) * P]] for c in range(8) for t in range(2)], T("inv_p"))
                pe.wait_ge(ada_out, N_ADA * l + N_ADA)
                for jj in range(N_ADA - ADA_BANKS, N_ADA):
                    ada_columns(l, jj)
                pe.wait_ge(scale_ready, norm + (N1_MIX + 1))
                spread(4, 0, 8)
                spread(6, 8, 8)
                pe.wait_ge(mix_ready, l + 1)
                pe.wait_ge(mods_ready, l + 1)
                for j in range(4):
                    panel1(l, P1_OUT + j, C1_OUT + 2 * j, mix1)
                norm_of_x(norm + N1_FFN, 2 * l + 2)
                with pe.Fori(0, 3) as i:
                    pe.wait_ge(h_ready, 16 * l + 16)
                    for j in range(6):
                        panel1(l, P1_FFN + j, C1_FFN + 2 * j, H1, turn=i, turn_c=3 * i)
                for j in range(18, 22):
                    panel1(l, P1_FFN + j, C1_FFN + 2 * j, H1)
                with pe.Fori(0, 2) as i:
                    pe.wait_ge(drained[3], out_of(l, C1_FFN + 43))
                    for j in range(6):
                        panel1(l, P1_DOWN + j, C1_DOWN + j // 3 * 2, hid1, turn=i, turn_c=i, part=KPARTS[j % 3], k_all=KF)
            norm_of_x(N_FINAL, 2 * DEPTH + 1)
            pe_second(pe, sums, spread, panel)


def kernel(**inputs):
    import concourse.bacc as bacc
    from concourse.bass_utils import run_bass_kernel_spmd

    a = {n: np.asarray(v) for n, v in inputs.items()}

    def columns(v):
        return np.ascontiguousarray(v.reshape(-1, P).T)

    def layers(pack):
        return np.stack([np.concatenate(pack(l), axis=1) for l in range(DEPTH)])

    def every(v):
        return np.broadcast_to(v[None, :], (P, v.shape[0]))

    def tokens(v):
        return np.ascontiguousarray(v[0].reshape(-1, KD, P).transpose(2, 1, 0))

    vec1 = layers(lambda l: [columns(a[n][l]) for n in ("norm1_g", "dn_conv_w", "sc_conv_w", "dn_norm_g", "sc_norm_g", "norm2_g")]
                  + [every(a["dn_a_log"][l]), every(a["dn_dt_bias"][l]), columns(a["b_ada_2"][l])])
    vec2 = layers(lambda l: [columns(a[n + "_2"][l]) for n in (
        "b_in", "q_gain", "k_gain", "conv_dw_w", "conv_dw_b", "conv_ln_g", "conv_ln_b", "conv_pw_b", "pool_scale", "b_out",
        "ln1_g", "ln1_b", "ln2_g", "ln2_b", "ffn_dw_w", "ffn_dw_b")])
    cond = np.stack([columns(a["c_2"]), columns(a["c_ctx_2"])], axis=2)
    arrays = {
        "x": tokens(a["x"]), "ctx_in": tokens(a["ctx_2"]), "cond": cond, "vec1": vec1, "vec_final": columns(a["final_norm_g"]),
        "vec2": np.concatenate(list(vec2), axis=1), "tabs": tables(), "counts": window_counts(), "w_in": a["w_in"], "w_out": a["w_out"],
        "w_gate": a["ffn_w_gate"], "w_up": a["ffn_w_up"], "w_down": a["ffn_w_down"], "w_ada": a["w_ada_2"], "w_in2": a["w_in_2"],
        "w_pool": a["pool_w_2"], "w_pw": a["conv_pw_w_2"], "w_out2": a["w_out_2"], "w_up2": a["w_up_2"], "w_down2": a["w_down_2"],
    }
    arrays = {n: np.ascontiguousarray(v) for n, v in arrays.items()}
    nc = bacc.Bacc("TRN2", target_bir_lowering=False, num_devices=1)
    args = {n: nc.dram_tensor(n, v.shape, F32, kind="ExternalInput").ap() for n, v in arrays.items()}
    out = nc.dram_tensor("out", (P, KD, SEQ), F32, kind="ExternalOutput").ap()
    build(nc, *args.values(), out)
    r = run_bass_kernel_spmd(nc, [arrays], core_ids=[0])
    return np.ascontiguousarray(r.results[0]["out"].transpose(2, 1, 0)).reshape(1, SEQ, D)
```
